# Optimizing a Trainium2 kernel written in Bass

```python
import jax, jax.numpy as jnp
from jax import lax
import numpy as np

D_MODEL = 1024
BATCH = 1
SEQ = 512
DEPTH = 2

N_HEADS = 16
HEAD_DIM = D_MODEL // N_HEADS
D_FF = -(-8 * D_MODEL // (3 * 256)) * 256
N_A_LAYERS = DEPTH // 2
N_B_LAYERS = DEPTH - N_A_LAYERS
BLOCK = 128
ROPE_THETA = 10000.0
NORM_EPS = 1e-6
DILATED_BRANCHES = ((128, 1), (512, 4), (2048, 16))


def _rmsnorm(h, g):
    hf = h.astype(jnp.float32)
    y = hf * lax.rsqrt(jnp.mean(hf * hf, axis=-1, keepdims=True) + NORM_EPS)
    return (y * g.astype(jnp.float32)).astype(h.dtype)

def _rope(a):
    s, d = a.shape[1], a.shape[3]
    inv_freq = ROPE_THETA ** (-jnp.arange(0, d, 2, dtype=jnp.float32) / d)
    ang = jnp.arange(s, dtype=jnp.float32)[:, None] * inv_freq[None, :]
    cos = jnp.cos(ang)[:, None, :]
    sin = jnp.sin(ang)[:, None, :]
    af = a.astype(jnp.float32)
    a1, a2 = af[..., : d // 2], af[..., d // 2:]
    return jnp.concatenate([a1 * cos - a2 * sin, a2 * cos + a1 * sin], axis=-1).astype(a.dtype)

def _swiglu(h, w_gate, w_up, w_down):
    return (jax.nn.silu(h @ w_gate) * (h @ w_up)) @ w_down

def _stick_breaking(q, k, v):
    b, s, h, d = q.shape
    nq = s // BLOCK
    scale = d ** -0.5
    kh = k.transpose(0, 2, 1, 3)
    vh = v.transpose(0, 2, 1, 3)
    qblk = q.reshape(b, nq, BLOCK, h, d).transpose(1, 0, 3, 2, 4)
    key_pos = jnp.arange(s)

    def one_block(args):
        qb, bi = args
        qpos = bi * BLOCK + jnp.arange(BLOCK)
        strict = key_pos[None, :] < qpos[:, None]
        z = jnp.einsum('bhqd,bhkd->bhqk', qb, kh).astype(jnp.float32) * scale
        log_stay = jnp.where(strict, jax.nn.log_sigmoid(-z), 0.0)
        log_after = lax.cumsum(log_stay, axis=3, reverse=True) - log_stay
        w = jnp.where(strict, jnp.exp(jax.nn.log_sigmoid(z) + log_after), 0.0)
        return jnp.einsum('bhqk,bhkd->bhqd', w, vh.astype(jnp.float32)).astype(q.dtype)

    out = lax.map(one_block, (qblk, jnp.arange(nq)))
    return out.transpose(1, 0, 3, 2, 4).reshape(b, s, h, d)

def _to_blocks(a, r):
    b, s, h, d = a.shape
    n = s // r
    nb = -(-n // BLOCK)
    a = a.reshape(b, n, r, h, d).transpose(0, 2, 3, 1, 4)
    a = jnp.pad(a, ((0, 0), (0, 0), (0, 0), (0, nb * BLOCK - n), (0, 0)))
    return a.reshape(b, r, h, nb, BLOCK, d)

def _from_blocks(a, s):
    b, r, h, nb, blk, e = a.shape
    n = s // r
    a = a.reshape(b, r, h, nb * blk, e)[:, :, :, :n]
    return a.transpose(0, 3, 1, 2, 4).reshape(b, s, h, e)

def _dilated_branch(qb, kb, vb, steps):
    nb = qb.shape[3]
    scale = qb.shape[-1] ** -0.5
    k_prev = jnp.concatenate([jnp.zeros_like(kb[:, :, :, :1]), kb[:, :, :, :-1]], axis=3)
    v_prev = jnp.concatenate([jnp.zeros_like(vb[:, :, :, :1]), vb[:, :, :, :-1]], axis=3)
    k_band = jnp.concatenate([k_prev, kb], axis=4)
    v_band = jnp.concatenate([v_prev, vb], axis=4)
    z = jnp.einsum('brhnqd,brhnkd->brhnqk', qb, k_band).astype(jnp.float32) * scale
    qi = jnp.arange(BLOCK)[:, None]
    kj = jnp.arange(2 * BLOCK)[None, :]
    dist = BLOCK + qi - kj
    key_idx = (jnp.arange(nb)[:, None, None] - 1) * BLOCK + kj[None]
    valid = (dist >= 0)[None] & (dist <= steps)[None] & (key_idx >= 0)
    z = jnp.where(valid, z, -jnp.inf)
    m = jnp.max(z, axis=-1, keepdims=True)
    p = jnp.exp(z - m)
    den = jnp.sum(p, axis=-1, keepdims=True)
    o = jnp.einsum('brhnqk,brhnkd->brhnqd', p, v_band.astype(jnp.float32)) / den
    lse = m + jnp.log(den)
    return o, lse

def _dilated_attention(q, kv_blocks):
    s = q.shape[1]
    outs, lses = [], []
    for (window, r), (kb, vb) in zip(DILATED_BRANCHES, kv_blocks):
        o, lse = _dilated_branch(_to_blocks(q, r), kb, vb, window // r)
        outs.append(_from_blocks(o, s))
        lses.append(_from_blocks(lse, s))
    wts = jax.nn.softmax(jnp.stack(lses, axis=0), axis=0)
    return jnp.sum(wts * jnp.stack(outs, axis=0), axis=0).astype(q.dtype)

def first_inputs(seed: int = 0) -> dict:
    key = jax.random.key(seed)
    ks = jax.random.split(key, 14)
    d, f = D_MODEL, D_FF
    nrm = lambda k, shape, fan: jax.random.normal(k, shape, jnp.float32) * fan ** -0.5
    gain = lambda k, shape: 1.0 + 0.02 * jax.random.normal(k, shape, jnp.float32)
    return {
        "x": jax.random.normal(ks[0], (BATCH, SEQ, d), jnp.float32),
        "norm_mix": gain(ks[1], (DEPTH, d)),
        "w_qkv_a": nrm(ks[2], (N_A_LAYERS, d, 3 * d), d),
        "w_o_a": nrm(ks[3], (N_A_LAYERS, d, d), d),
        "norm_kv": gain(ks[4], (d,)),
        "w_kv": nrm(ks[5], (d, 2 * d), d),
        "w_q_b": nrm(ks[6], (N_B_LAYERS, d, d), d),
        "w_o_b": nrm(ks[7], (N_B_LAYERS, d, d), d),
        "norm_ffn": gain(ks[8], (DEPTH, d)),
        "w_gate": nrm(ks[9], (DEPTH, d, f), d),
        "w_up": nrm(ks[10], (DEPTH, d, f), d),
        "w_down": nrm(ks[11], (DEPTH, f, d), f),
        "norm_final": gain(ks[12], (d,)),
    }

def first_block(x, norm_mix, w_qkv_a, w_o_a, norm_kv, w_kv, w_q_b, w_o_b,
              norm_ffn, w_gate, w_up, w_down, norm_final):
    b, s, d = x.shape
    h = x
    kv_blocks = None
    for layer in range(DEPTH):
        hn = _rmsnorm(h, norm_mix[layer])
        if layer < N_A_LAYERS:
            q, k, v = jnp.split(hn @ w_qkv_a[layer], 3, axis=-1)
            q = q.reshape(b, s, N_HEADS, HEAD_DIM)
            k = k.reshape(b, s, N_HEADS, HEAD_DIM)
            v = v.reshape(b, s, N_HEADS, HEAD_DIM)
            o = _stick_breaking(q, k, v).reshape(b, s, d)
            h = h + o @ w_o_a[layer]
        else:
            j = layer - N_A_LAYERS
            if layer == N_A_LAYERS:
                kv = _rmsnorm(h, norm_kv) @ w_kv
                ks_, vs_ = jnp.split(kv, 2, axis=-1)
                ks_ = _rope(ks_.reshape(b, s, N_HEADS, HEAD_DIM))
                vs_ = vs_.reshape(b, s, N_HEADS, HEAD_DIM)
                kv_blocks = tuple((_to_blocks(ks_, r), _to_blocks(vs_, r))
                                  for (_, r) in DILATED_BRANCHES)
            q = _rope((hn @ w_q_b[j]).reshape(b, s, N_HEADS, HEAD_DIM))
            o = _dilated_attention(q, kv_blocks).reshape(b, s, d)
            h = h + o @ w_o_b[j]
        h = h + _swiglu(_rmsnorm(h, norm_ffn[layer]), w_gate[layer], w_up[layer], w_down[layer])
    return _rmsnorm(h, norm_final)


DEPTH_2 = 1

CHUNK = 64
D_SHORT = D_MODEL
D_CONF = D_MODEL
SHORT_K = 3
CONF_K = 31
D_FF_2 = -(-8 * D_MODEL // (3 * 256)) * 256
N_MOD = 6
EPS = 1e-6
LN_EPS = 1e-5
SPLITS = (D_SHORT, 2 * D_SHORT, 3 * D_SHORT,
          3 * D_SHORT + D_CONF, 3 * D_SHORT + 2 * D_CONF,
          3 * D_SHORT + 2 * D_CONF + D_MODEL)
D_IN = 3 * D_SHORT + 2 * D_CONF + 2 * D_MODEL


def rms_norm(x, g):
    xf = x.astype(jnp.float32)
    y = xf * lax.rsqrt(jnp.mean(xf * xf, axis=-1, keepdims=True) + EPS)
    return (y * g.astype(jnp.float32)).astype(x.dtype)

def layer_norm(x, g, b):
    xf = x.astype(jnp.float32)
    mu = jnp.mean(xf, axis=-1, keepdims=True)
    var = jnp.mean(jnp.square(xf - mu), axis=-1, keepdims=True)
    y = (xf - mu) * lax.rsqrt(var + LN_EPS)
    return (y * g.astype(jnp.float32) + b.astype(jnp.float32)).astype(x.dtype)

def causal_dwconv(u, w):
    k, ch = w.shape
    return lax.conv_general_dilated(
        u, w.astype(u.dtype)[:, None, :], window_strides=(1,), padding=[(k - 1, 0)],
        dimension_numbers=('NWC', 'WIO', 'NWC'), feature_group_count=ch)

def second_inputs(seed: int = 0) -> dict:
    key = jax.random.key(seed)
    ks = jax.random.split(key, 20)
    n = jax.random.normal
    d = D_MODEL
    return {
        'x': n(ks[0], (BATCH, SEQ, d), jnp.float32),
        'c': n(ks[1], (BATCH, d), jnp.float32),
        'w_ada': n(ks[2], (DEPTH_2, d, N_MOD * d), jnp.float32) * (0.5 * d ** -0.5),
        'b_ada': n(ks[3], (DEPTH_2, N_MOD * d), jnp.float32) * 0.02,
        'norm_mix_g': 1.0 + 0.05 * n(ks[4], (DEPTH_2, d), jnp.float32),
        'w_in': n(ks[5], (DEPTH_2, d, D_IN), jnp.float32) * d ** -0.5,
        'conv_short_w': n(ks[6], (DEPTH_2, SHORT_K, D_SHORT), jnp.float32) * SHORT_K ** -0.5,
        'w_short_out': n(ks[7], (DEPTH_2, D_SHORT, d), jnp.float32) * D_SHORT ** -0.5,
        'conv_conf_w': n(ks[8], (DEPTH_2, CONF_K, D_CONF), jnp.float32) * CONF_K ** -0.5,
        'conv_conf_b': n(ks[9], (DEPTH_2, D_CONF), jnp.float32) * 0.02,
        'conf_ln_g': 1.0 + 0.05 * n(ks[10], (DEPTH_2, D_CONF), jnp.float32),
        'conf_ln_b': n(ks[11], (DEPTH_2, D_CONF), jnp.float32) * 0.02,
        'w_conf_out': n(ks[12], (DEPTH_2, D_CONF, d), jnp.float32) * D_CONF ** -0.5,
        'w_o': n(ks[13], (DEPTH_2, d, d), jnp.float32) * d ** -0.5,
        'norm_ffn_g': 1.0 + 0.05 * n(ks[14], (DEPTH_2, d), jnp.float32),
        'w_ffn_in': n(ks[15], (DEPTH_2, d, 2 * D_FF_2), jnp.float32) * d ** -0.5,
        'w_ffn_out': n(ks[16], (DEPTH_2, D_FF_2, d), jnp.float32) * D_FF_2 ** -0.5,
        'final_norm_g': 1.0 + 0.05 * n(ks[17], (d,), jnp.float32),
    }

def second_block(x, c, w_ada, b_ada, norm_mix_g, w_in, conv_short_w, w_short_out,
              conv_conf_w, conv_conf_b, conf_ln_g, conf_ln_b, w_conf_out, w_o,
              norm_ffn_g, w_ffn_in, w_ffn_out, final_norm_g):
    for l in range(DEPTH_2):
        mod = jax.nn.silu(c) @ w_ada[l] + b_ada[l]
        sh1, sc1, g1, sh2, sc2, g2 = jnp.split(mod[:, None, :], N_MOD, axis=-1)

        h = rms_norm(x, norm_mix_g[l]) * (1.0 + sc1) + sh1
        proj = jnp.einsum('bsd,de->bse', h, w_in[l])
        b_s, c_s, v_s, v_c, gl_c, gate_br = jnp.split(proj, SPLITS[:-1], axis=-1)

        y_a = b_s * causal_dwconv(c_s * v_s, conv_short_w[l])
        y_a = jnp.einsum('bsc,cd->bsd', y_a, w_short_out[l])

        u = v_c * jax.nn.sigmoid(gl_c)
        u = causal_dwconv(u, conv_conf_w[l]) + conv_conf_b[l]
        u = jax.nn.silu(layer_norm(u, conf_ln_g[l], conf_ln_b[l]))
        y_b = jnp.einsum('bsc,cd->bsd', u, w_conf_out[l])

        g_a, g_b = jnp.split(jax.nn.sigmoid(gate_br), 2, axis=-1)
        mix = jnp.einsum('bsd,de->bse', g_a * y_a + g_b * y_b, w_o[l])
        x = x + g1 * mix

        h2 = rms_norm(x, norm_ffn_g[l]) * (1.0 + sc2) + sh2
        a, bgate = jnp.split(jnp.einsum('bsd,df->bsf', h2, w_ffn_in[l]), 2, axis=-1)
        x = x + g2 * jnp.einsum('bsf,fd->bsd', jax.nn.silu(a) * bgate, w_ffn_out[l])

    return rms_norm(x, final_norm_g)


def setup_inputs(seed=0):
    out = dict(first_inputs(seed))
    for name, value in second_inputs(seed + 1).items():
        if name != "x":
            out[name + "_2"] = value
    return out


def reference(
    x, norm_mix, w_qkv_a, w_o_a, norm_kv, w_kv, w_q_b, w_o_b, norm_ffn, w_gate, w_up, w_down,
    norm_final, c_2, w_ada_2, b_ada_2, norm_mix_g_2, w_in_2, conv_short_w_2, w_short_out_2,
    conv_conf_w_2, conv_conf_b_2, conf_ln_g_2, conf_ln_b_2, w_conf_out_2, w_o_2, norm_ffn_g_2,
    w_ffn_in_2, w_ffn_out_2, final_norm_g_2,
):
    x = first_block(
        x, norm_mix, w_qkv_a, w_o_a, norm_kv, w_kv, w_q_b, w_o_b, norm_ffn, w_gate, w_up,
        w_down, norm_final,
    )
    return second_block(
        x, c_2, w_ada_2, b_ada_2, norm_mix_g_2, w_in_2, conv_short_w_2, w_short_out_2,
        conv_conf_w_2, conv_conf_b_2, conf_ln_g_2, conf_ln_b_2, w_conf_out_2, w_o_2,
        norm_ffn_g_2, w_ffn_in_2, w_ffn_out_2, final_norm_g_2,
    )


_drawn_inputs = setup_inputs


def setup_inputs(seed=0):
    import zlib

    import numpy as np

    out = dict(_drawn_inputs(seed))
    spreads = {}
    factors = {'norm_mix': 3.285,
     'norm_kv': 8.0,
     'norm_ffn': 2.92,
     'norm_final': 2.728,
     'norm_mix_g_2': 3.016,
     'conv_conf_b_2': 27.103,
     'conf_ln_g_2': 51.937,
     'conf_ln_b_2': 183.037,
     'norm_ffn_g_2': 3.701}
    for name, (base, spread) in spreads.items():
        noise = np.random.default_rng([zlib.crc32(name.encode()), seed]).standard_normal(out[name].shape)
        drawn = base * np.exp(spread * noise) if base else spread * noise
        out[name] = __import__('jax').numpy.asarray(drawn.astype(out[name].dtype))
    for name, factor in factors.items():
        out[name] = (out[name] * factor).astype(out[name].dtype)
    return out
```

```python
from contextlib import ExitStack

import numpy as np

import concourse.bass as bass
from concourse import mybir

F32 = mybir.dt.float32
F32R = mybir.dt.float32r
BF16 = mybir.dt.bfloat16
ALU = mybir.AluOpType
ACT = mybir.ActivationFunctionType

P = 128
SEQ = 512
D = 1024
KD = D // P
HEADS = 16
HD = 64
PAIRS = HEADS // 2
DFF = 2816
FT = DFF // P
PARTS = (8, 8, 6)
SHORT_K = 3
CONF_K = 31
EPS = 1e-6
LN_EPS = 1e-5
BLK = 128
NB = SEQ // BLK
NEG = -1e30

U_QKV = (0, 50)
U_WO = (12, 62)
U_FFN = (16, 66, 140)
U_CONF, U_SHORT, U_GA, U_GB, U_CO, U_OUT = 100, 108, 120, 128, 132, 136
U_END = U_FFN[2] + (2 * FT + len(PARTS) * KD) // 2

CHUNKS = ((0, 384), (384, 768), (768, 1280))
OFF_K = {3: 0, 2: 128, 1: 384, 0: 768}
OFF_Q = {0: 0, 1: 128, 2: 384, 3: 768}
TRI = 1280

C_ID, C_ONE, C_NTRI, C_NONE, C_MASK, C_PERM, C_COS, C_SIN, C_COUNT = 0, 128, 256, 384, 512, 640, 768, 1280, 1792
C_ALL = C_COUNT + TRI
V_MIX0, V_MIX1, V_KV, V_FFN0, V_FFN1, V_FIN, V_MIX2, V_CB, V_LG, V_LB, V_FFN2, V_FIN2, V_C, V_ADA = (
    0, 8, 16, 24, 32, 40, 48, 56, 64, 72, 80, 88, 96, 104)
V_SW = V_ADA + 48
V_CW = V_SW + KD * SHORT_K
V_ALL = V_CW + KD * CONF_K
M_SH1, M_SC1, M_G1, M_SH2, M_SC2, M_G2 = 0, 8, 16, 24, 32, 40

HALVES = ((range(0, 13), range(26, 28)), (range(13, 26), range(28, 31)))
ND = sum(len(a) for a, _ in HALVES)
NP_OPS = 2 * (CONF_K - ND) - 1


def constants():
    t = np.zeros((P, C_ALL), np.float32)
    i, j = np.arange(P)[:, None], np.arange(P)[None, :]
    t[:, C_ID:C_ID + P] = i == j
    t[:, C_ONE:C_ONE + P] = 1.0
    t[:, C_NTRI:C_NTRI + P] = -(i >= j).astype(np.float32)
    t[:, C_NONE:C_NONE + P] = -1.0
    t[:, C_MASK:C_MASK + P] = np.where(i < j, 0.0, NEG)
    half = HD // 2
    for m in range(P):
        head, r = divmod(m, HD)
        if r < half:
            t[head * HD + r + half, C_PERM + m] = -1.0
        else:
            t[head * HD + r - half, C_PERM + m] = 1.0
    freq = (np.float32(10000.0) ** (-np.arange(0, HD, 2, dtype=np.float32) / np.float32(HD))).astype(np.float32)
    angle = (np.arange(SEQ, dtype=np.float32)[None, :] * freq[:, None]).astype(np.float32)
    t[:, C_COS:C_COS + SEQ] = np.tile(np.cos(angle), (4, 1))
    t[:, C_SIN:C_SIN + SEQ] = np.tile(np.sin(angle), (4, 1))
    for b in range(NB):
        q = b * BLK + np.arange(P)[:, None]
        k = np.arange(BLK * (b + 1))[None, :]
        dist = q - k
        n = (((dist >= 0) & (dist <= 128)).astype(np.int64)
             + ((dist >= 0) & (dist % 4 == 0)) + ((dist >= 0) & (dist % 16 == 0)))
        t[:, C_COUNT + OFF_Q[b]:C_COUNT + OFF_Q[b] + BLK * (b + 1)] = np.where(
            n > 0, np.log(np.maximum(n, 1).astype(np.float64)), NEG)
    return t


def wait(eng, sem, value):
    if isinstance(value, int) and value <= 0:
        return
    eng.wait_ge(sem, value)


def wait_apart(eng, sem, value, passed):
    eng.wait_ge(sem, value)
    if not isinstance(value, int):
        eng.sem_inc(passed, 1)


def loop(eng, lo, hi, body, peel=False):
    if peel:
        body(lo)
        lo += 1
    with eng.Fori(lo, hi) as i:
        body(i)


def build_program(nc, x_t, const_d, vec_d, stream, ada_w, out_t):
    with ExitStack() as ctx:
        def sb(name, shape, dt=F32, stack=ctx):
            return stack.enter_context(nc.sbuf_tensor(name, shape, dt))

        def sem(name):
            return ctx.enter_context(nc.semaphore(name))

        h = sb("h", [P, KD, SEQ])
        xh, xl = sb("xh", [P, KD, SEQ], F32R), sb("xl", [P, KD, SEQ], F32R)
        yh, yl = sb("yh", [P, KD, SEQ], F32R), sb("yl", [P, KD, SEQ], F32R)
        raw = [sb(f"raw{s}", [P, KD, P]) for s in range(2)]
        wh = [sb(f"wh{s}", [P, KD, P], F32R) for s in range(2)]
        wl = [sb(f"wl{s}", [P, KD, P], F32R) for s in range(2)]
        con = sb("con", [P, C_ALL])
        vec = sb("vec", [P, V_ALL])
        ntri, nones = sb("ntri", [P, P], F32R), sb("nones", [P, P], F32R)
        idb, maskb = sb("idb", [P, P], BF16), sb("maskb", [P, P], BF16)
        rstd = sb("rstd", [P, SEQ])
        ssum = sb("ssum", [P, SEQ])
        sq = [sb(f"sq{s}", [P, SEQ]) for s in range(2)]
        tmp = [sb(f"tmp{s}", [P, SEQ]) for s in range(2)]
        modc = sb("modc", [P, 48])
        cs = sb("cs", [P, KD])
        small = sb("small", [P, 16])
        var4, root4 = sb("var4", [P, NB]), sb("root4", [P, NB])
        gmc = sb("gmc", [P, 16])
        mhalf = sb("mhalf", [P, 1])

        with ExitStack() as r:
            sph, spl, wa = sb("sph", [P, TRI], F32R, r), sb("spl", [P, TRI], F32R, r), sb("wa", [P, TRI], F32, r)
        with ExitStack() as r:
            ma, sgb = sb("ma", [P, KD, SEQ], F32, r), sb("sgb", [P, KD, SEQ], F32, r)
        x2h, x2l = sb("x2h", [P, KD, SEQ], F32R), sb("x2l", [P, KD, SEQ], F32R)

        with ExitStack() as r:
            qh = [sb(f"qh{i}", [P, SEQ], F32R, r) for i in range(2)]
            ql = [sb(f"ql{i}", [P, SEQ], F32R, r) for i in range(2)]
            kh = [sb(f"kh{i}", [P, SEQ], F32R, r) for i in range(2)]
            kl = [sb(f"kl{i}", [P, SEQ], F32R, r) for i in range(2)]
            qkv = [sb(f"qkv{i}", [P, SEQ], F32, r) for i in range(3)]
            vn = [sb(f"vn{i}", [P, NB, P], F32, r) for i in range(2)]
            ez, sp = sb("ez", [P, TRI], F32, r), sb("sp", [P, TRI], F32, r)
        with ExitStack() as r:
            gs, us, si, af = [sb(n, [P, SEQ], F32, r) for n in ("gs", "us", "si", "af")]
            araw = [sb(f"araw{s}", [P, KD, P], F32, r) for s in range(2)]
            aprod = sb("aprod", [P, KD, P], F32, r)
            asum = [sb(f"asum{s}", [P, P], F32, r) for s in range(2)]
        PADC = CONF_K - 1
        PADS = SHORT_K - 1
        cin = sb("cin", [P, KD, PADC + SEQ])
        acc = sb("acc", [P, KD, SEQ])
        csb, sgt = sb("csb", [P, SEQ]), sb("sgt", [P, SEQ])
        cv = sb("cv", [P, PADS + SEQ])

        G = [ctx.enter_context(nc.psum_tensor(f"G{s}", [P, SEQ], F32)) for s in range(2)]
        Z = [ctx.enter_context(nc.psum_tensor(f"Z{s}", [P, SEQ], F32)) for s in range(3)]
        O = ctx.enter_context(nc.psum_tensor("O", [P, SEQ], F32))
        T = ctx.enter_context(nc.psum_tensor("T", [P, SEQ], F32))
        M = ctx.enter_context(nc.psum_tensor("M", [P, SEQ], F32))

        in_h, in_vec, in_con = sem("in_h"), sem("in_vec"), sem("in_con")
        landed = [sem("landed0"), sem("landed1")]
        w_hi, w_lo = sem("w_hi"), sem("w_lo")
        used = sem("used")
        evac = [sem("evac0"), sem("evac1")]
        consts = sem("consts")
        cs_ready = sem("cs_ready")
        ss_clear = sem("ss_clear")
        sq_ready, sq_added = sem("sq_ready"), sem("sq_added")
        stat = sem("stat")
        var_ready, root_ready = sem("var_ready"), sem("root_ready")
        diag_ready, spread = sem("diag_ready"), sem("spread")
        rstd_ready = sem("rstd_ready")
        mod_t = sem("mod_t")
        x_hi, x_lo = sem("x_hi"), sem("x_lo")
        x2_hi, x2_lo = sem("x2_hi"), sem("x2_lo")
        z_done, z_abs, z_exp, z_ln = sem("z_done"), sem("z_abs"), sem("z_exp"), sem("z_ln")
        sp_ready, sp_hi, sp_lo, cum = sem("sp_ready"), sem("sp_hi"), sem("sp_lo"), sem("cum")
        w_exp = sem("w_exp")
        pv_done = sem("pv_done")
        qk_hi, qk_lo = sem("qk_hi"), sem("qk_lo")
        v_tr, v_nat = sem("v_tr"), sem("v_nat")
        perm, rot = sem("perm"), sem("rot")
        roped_c, roped = sem("roped_c"), sem("roped")
        o_hi, o_lo = sem("o_hi"), sem("o_lo")
        zmax, zneg, p_exp, rden = sem("zmax"), sem("zneg"), sem("p_exp"), sem("rden")
        p_norm, p_tr = sem("p_norm"), sem("p_tr")
        p_cp_a, p_cp_d = sem("p_cp_a"), sem("p_cp_d")
        silu, a_raw, a_hi, a_lo = sem("silu"), sem("a_raw"), sem("a_hi"), sem("a_lo")
        ada_land = [sem("ada_land0"), sem("ada_land1")]
        ada_fold, ada_sum, ada_mm = sem("ada_fold"), sem("ada_sum"), sem("ada_mm")
        modc_ready, gmc_ready, y_ready = sem("modc_ready"), sem("gmc_ready"), sem("y_ready")
        padded = sem("padded")
        tap_d, tap_p = sem("tap_d"), sem("tap_p")
        u_ready, u_added = sem("u_ready"), sem("u_added")
        s_tap = sem("s_tap")
        s_hi, s_lo = sem("s_hi"), sem("s_lo")
        mean_ready, centred, ln_t, ln_s, u_hi, u_lo = [
            sem(n) for n in ("mean_ready", "centred", "ln_t", "ln_s", "u_hi", "u_lo")]
        mix_t, mix_hi, mix_lo = sem("mix_t"), sem("mix_hi"), sem("mix_lo")
        done, stored = sem("done"), sem("stored")
        passed = sem("passed")

        block = ctx.enter_context(nc.Block())

        def f32(ap):
            return ap.bitcast(F32)

        def tile(buf, n):
            return buf[:, n, :] if isinstance(n, int) else buf[:, bass.ds(n, 1), :].rearrange("p a s -> p (a s)")

        def col(buf, n):
            return buf[:, n:n + 1] if isinstance(n, int) else buf[:, bass.ds(n, 1)]

        ident = con[:, C_ID:C_ID + P]
        ones = con[:, C_ONE:C_ONE + P]

        Q_IN, Q_FFN0, Q_MID, Q_FFN1, Q_FIN, Q_MIX2, Q_VAR, Q_FFN2, Q_OUT = range(9)
        S_IN, S_FFN0, S_MID, S_FFN1, S_FIN, S_MIX2, S_MEAN, S_VAR, S_FFN2, S_OUT = range(10)

        @block.sync
        def _(eng):
            def load(u, s):
                wait(eng, w_lo, 2 * (u - 1) + s + 1)
                g = 2 * u + s
                src = stream[g] if isinstance(g, int) else stream[bass.ds(g, 1)].rearrange("a p k c -> (a p) k c")
                eng.dma_start(raw[s][:, :, :], src).then_inc(landed[s], 16)

            eng.dma_start(h[:, :, :], x_t).then_inc(in_h, 16)
            eng.dma_start(vec[:, :], vec_d).then_inc(in_vec, 16)
            load(0, 0)
            load(0, 1)
            eng.dma_start(con[:, :], const_d).then_inc(in_con, 16)
            at = 1
            for which in range(2):
                u = U_FFN[which]
                for part, nt in enumerate(PARTS):
                    with eng.Fori(at, u + nt) as v:
                        load(v, 0)
                        load(v, 1)
                    u += nt
                    idx = 12 * which + 4 * part - u

                    def with_ada(v):
                        for s in range(2):
                            load(v, s)
                            j = 2 * (v + idx) + s
                            wait(eng, ada_sum, j - 1)
                            src = ada_w[j] if isinstance(j, int) else ada_w[bass.ds(j, 1)].rearrange("a p k c -> (a p) k c")
                            eng.dma_start(araw[s][:, :, :], src).then_inc(ada_land[s], 16)
                    loop(eng, u, u + KD // 2, with_ada, peel=which + part == 0)
                    u += KD // 2
                    at = u
            with eng.Fori(at, U_END) as v:
                load(v, 0)
                load(v, 1)
            for n in range(KD):
                eng.wait_ge(done, n + 1)
                eng.dma_start(out_t[:, n, :], h[:, n, :]).then_inc(stored, 16)
            eng.wait_ge(stored, 16 * KD)

        @block.scalar
        def _(eng):
            def split_hi(u, s):
                if isinstance(u, int) and u >= U_END:
                    return
                wait(eng, landed[s], 16 * (u + 1))
                wait(eng, used, 2 * (u - 1) + s + 1)
                eng.activation(wh[s][:, :, :], raw[s][:, :, :], ACT.Copy).then_inc(w_hi, 1)

            def square(n, s, count, src, ready, value):
                wait_apart(eng, ready, value, passed)
                if not isinstance(count, int) or count > 1:
                    wait_apart(eng, sq_added, count - 1, passed)
                eng.activation(sq[s][:, :], tile(src, n), ACT.Square).then_inc(sq_ready, 1)

            def residual(u0, rnd, gains=None, gains2=None, last=False):
                def pair(u):
                    for s in range(2):
                        n = 2 * (u - u0) + s
                        split_hi(u + 1, s)
                        wait_apart(eng, evac[s], u + 1, passed)
                        if gains is not None:
                            eng.activation(tile(xh, n), tile(h, n), ACT.Copy,
                                           scale=col(vec, gains + n)).then_inc(x_hi, 1)
                        if gains2 is not None:
                            eng.activation(tile(x2h, n), tile(h, n), ACT.Copy,
                                           scale=col(vec, gains2 + n)).then_inc(x2_hi, 1)
                        square(n, s, 8 * rnd + n, h, evac[s], u + 1)
                with eng.Fori(u0, u0 + KD // 2 - last) as u:
                    pair(u)
                if last:
                    pair(u0 + KD // 2 - 1)

            def attention(layer):
                base = PAIRS * layer

                def slot(i, par, gemm=True, attn=True):
                    p = 2 * i + par
                    a, gp = p - 1, p + base

                    def step(j):
                        g = 3 * par + j
                        return U_QKV[layer] + 3 * i + g // 2, g % 2

                    def split(j):
                        if gemm:
                            u, s = step(j)
                            split_hi(u + 1, s)

                    def scores_a(hh):
                        n = 3 * (2 * a + hh)
                        for c, (lo, hi) in enumerate(CHUNKS):
                            eng.wait_ge(z_done, n + c + 1)
                            eng.activation(ez[:, lo:hi], Z[c][:, 0:hi - lo], ACT.Abs).then_inc(z_abs, 1)
                        for c, (lo, hi) in enumerate(CHUNKS):
                            eng.wait_ge(z_abs, n + c + 1)
                            eng.activation(ez[:, lo:hi], ez[:, lo:hi], ACT.Exp, scale=-1.0).then_inc(z_exp, 1)
                        for c, (lo, hi) in enumerate(CHUNKS):
                            eng.wait_ge(z_exp, n + c + 1)
                            eng.activation(ez[:, lo:hi], ez[:, lo:hi], ACT.Ln, bias=1.0).then_inc(z_ln, 1)

                    def weights_a(hh):
                        n = 3 * (2 * a + hh)
                        for c, (lo, hi) in enumerate(CHUNKS):
                            eng.wait_ge(cum, n + c + 1)
                            eng.activation(wa[:, lo:hi], Z[c][:, 0:hi - lo], ACT.Exp).then_inc(w_exp, 1)

                    def exp_b(hh):
                        eng.wait_ge(zneg, 2 * a + hh + 1)
                        for b in range(NB):
                            o, w = OFF_Q[b], BLK * (b + 1)
                            eng.activation(ez[:, o:o + w], sp[:, o:o + w], ACT.Exp, bias=small[:, 4 + b:5 + b],
                                           accum_out=small[:, 8 + b:9 + b]).then_inc(p_exp, 1)

                    def copy_b(hh):
                        for c in (0, 2):
                            lo, hi = CHUNKS[c]
                            eng.wait_ge(p_tr, 3 * (2 * a + hh) + c + 1)
                            eng.activation(sp[:, lo:hi], Z[c][:, 0:hi - lo], ACT.Copy).then_inc(p_cp_a, 1)

                    def copy_hi(dst, j):
                        if layer == 0:
                            u, s = step(j)
                            eng.wait_ge(evac[s], u + 1)
                        else:
                            eng.wait_ge(roped, 2 * p + j + 1)
                        eng.activation(dst[par][:, :], qkv[j][:, :], ACT.Copy).then_inc(qk_hi, 1)

                    def values():
                        eng.wait_ge(v_tr, gp)
                        eng.activation(vn[1 - par][:, :, :].rearrange("p b d -> p (b d)"), T[:, :],
                                       ACT.Copy).then_inc(v_nat, 1)

                    def out_hi():
                        wait_apart(eng, pv_done, 2 * gp, passed)
                        eng.activation(tile(yh, a), O[:, :], ACT.Copy).then_inc(o_hi, 1)

                    if layer == 0:
                        if attn:
                            scores_a(0)
                        split(0)
                        if attn:
                            weights_a(0)
                            values()
                        if gemm:
                            copy_hi(qh, 0)
                        if attn:
                            scores_a(1)
                        split(1)
                        if gemm:
                            copy_hi(kh, 1)
                        if attn:
                            weights_a(1)
                        split(2)
                        if attn:
                            out_hi()
                    else:
                        if attn:
                            exp_b(0)
                            values()
                        split(0)
                        if attn:
                            copy_b(0)
                        if gemm:
                            copy_hi(qh, 0)
                        if attn:
                            exp_b(1)
                        split(1)
                        if attn:
                            copy_b(1)
                        split(2)
                        if gemm:
                            copy_hi(kh, 1)
                        if attn:
                            out_hi()

                slot(0, 0, attn=False)
                with eng.Fori(0, PAIRS // 2 - 1) as i:
                    slot(i, 1)
                    slot(i + 1, 0)
                slot(PAIRS // 2 - 1, 1)
                slot(PAIRS // 2, 0, gemm=False)

            def ffn(which, hid, last):
                u, f = U_FFN[which], FT * which
                for part, nt in enumerate(PARTS):
                    with eng.Fori(u, u + nt) as v:
                        n = v - u
                        split_hi(v + 1, 0)
                        if which < 2:
                            eng.wait_ge(evac[0], v + 1)
                            eng.activation(si[:, :], gs[:, :], ACT.Silu).then_inc(silu, 1)
                            split_hi(v + 1, 1)
                            wait_apart(eng, a_raw, n + f + 1, passed)
                            eng.activation(tile(hid, n), af[:, :], ACT.Copy).then_inc(a_hi, 1)
                        else:
                            eng.wait_ge(used, 2 * v + 1)
                            eng.wait_ge(evac[1], v)
                            eng.activation(sgt[:, :], G[0][:, :], ACT.Silu).then_inc(evac[0], 1)
                            split_hi(v + 1, 1)
                            wait_apart(eng, evac[1], v + 1, passed)
                            eng.activation(tile(hid, n), csb[:, :], ACT.Copy).then_inc(a_hi, 1)
                    u, f = u + nt, f + nt
                    if part < len(PARTS) - 1:
                        with eng.Fori(u, u + KD // 2) as v:
                            split_hi(v + 1, 0)
                            split_hi(v + 1, 1)
                    else:
                        last(u)
                    u += KD // 2

            def modulated(shift, dst, before):
                with eng.Fori(0, KD // 2) as i:
                    for s in range(2):
                        n = 2 * i + s
                        wait_apart(eng, mod_t, n + before + 1, passed)
                        eng.activation(tile(dst, n), tmp[s][:, :], ACT.Identity,
                                       bias=col(modc, shift + n)).then_inc(x_hi, 1)

            eng.wait_ge(in_vec, 16)
            eng.activation(cs[:, :], vec[:, V_C:V_C + KD], ACT.Silu).then_inc(cs_ready, 1)
            eng.wait_ge(in_h, 16)
            for n in range(KD):
                if n < 2:
                    split_hi(0, n)
                eng.activation(xh[:, n, :], h[:, n, :], ACT.Copy,
                               scale=vec[:, V_MIX0 + n:V_MIX0 + n + 1]).then_inc(x_hi, 1)
                square(n, n % 2, n, h, in_h, 16)
            eng.preload_act_table_set("natural_log_exp_and_others")
            attention(0)
            residual(U_WO[0], Q_FFN0, V_FFN0)
            ffn(0, yh, lambda u: residual(u, Q_MID, V_MIX1, V_KV))
            eng.preload_act_table_set("natural_log_exp_and_others")
            attention(1)
            residual(U_WO[1], Q_FFN1, V_FFN1)
            ffn(1, yh, lambda u: residual(u, Q_FIN))
            for n in range(KD):
                square(n, n % 2, 8 * Q_MIX2 + n, h, y_ready, n + 1)
            modulated(M_SH1, xh, 0)
            with eng.Fori(U_CONF, U_CONF + KD) as u:
                split_hi(u + 1, 0)
                split_hi(u + 1, 1)
                eng.wait_ge(used, 2 * u + 2)
                eng.wait_ge(evac[0], u)
                eng.activation(sgt[:, :], G[1][:, :], ACT.Sigmoid).then_inc(evac[1], 1)
            with eng.Fori(0, KD // 2) as i:
                for par in range(2):
                    def step(j):
                        g = 3 * par + j
                        return U_SHORT + 3 * i + g // 2, g % 2
                    u, s = step(0)
                    split_hi(u + 1, s)
                    eng.wait_ge(used, 2 * u + s + 1)
                    up, sp_ = step(-2)
                    eng.wait_ge(evac[sp_], up + 1)
                    eng.activation(csb[:, :], G[s][:, :], ACT.Copy).then_inc(evac[s], 1)
                    for j in (1, 2):
                        u, s = step(j)
                        split_hi(u + 1, s)
                    wait_apart(eng, evac[s], u + 1, passed)
                    eng.activation(tile(yh, 2 * i + par), sq[0][:, :], ACT.Copy).then_inc(s_hi, 1)
            with eng.Fori(U_GA, U_GA + KD) as u:
                split_hi(u + 1, 0)
                eng.wait_ge(used, 2 * u + 1)
                eng.wait_ge(evac[1], u)
                eng.activation(sgt[:, :], G[0][:, :], ACT.Sigmoid).then_inc(evac[0], 1)
                split_hi(u + 1, 1)
            with eng.Fori(U_GB, U_GB + KD // 2) as u:
                for s in range(2):
                    n = 2 * (u - U_GB) + s
                    split_hi(u + 1, s)
                    wait_apart(eng, used, 2 * u + s + 1, passed)
                    eng.activation(tile(sgb, n), G[s][:, :], ACT.Sigmoid).then_inc(evac[s], 1)
                    square(n, s, 8 * Q_VAR + n, acc, centred, n + 1)
            for n in range(KD):
                eng.wait_ge(ln_t, n + 1)
                eng.activation(acc[:, n, :], acc[:, n, :], ACT.Silu, scale=vec[:, V_LG + n:V_LG + n + 1],
                               bias=vec[:, V_LB + n:V_LB + n + 1]).then_inc(ln_s, 1)
                eng.wait_ge(ln_s, n + 1)
                eng.activation(yh[:, n, :], acc[:, n, :], ACT.Copy).then_inc(u_hi, 1)
            with eng.Fori(U_CO, U_CO + KD // 2) as u:
                for s in range(2):
                    n = 2 * (u - U_CO) + s
                    split_hi(u + 1, s)
                    wait_apart(eng, mix_t, n + 1, passed)
                    eng.activation(tile(xh, n), tmp[s][:, :], ACT.Copy).then_inc(mix_hi, 1)
            residual(U_OUT, Q_FFN2)
            modulated(M_SH2, yh, KD)
            ffn(2, xh, lambda u: residual(u, Q_OUT, last=True))

        @block.vector
        def _(eng):
            def split_lo(u, s):
                if isinstance(u, int) and u >= U_END:
                    return
                eng.wait_ge(w_hi, 2 * u + s + 1)
                eng.tensor_tensor(wl[s][:, :, :], raw[s][:, :, :], f32(wh[s][:, :, :]), ALU.subtract).then_inc(w_lo, 1)

            def operand_lo(hi, lo, n, gain, hi_sem, lo_sem, count):
                eng.wait_ge(hi_sem, count + 1)
                eng.scalar_tensor_tensor(tile(lo, n), tile(h, n), gain, f32(tile(hi, n)), ALU.mult,
                                         ALU.subtract).then_inc(lo_sem, 1)

            def residual(u0, gate=None, x_before=None, x2_before=None, gains=None, gains2=None, last=False):
                def pair(u):
                    for s in range(2):
                        n = 2 * (u - u0) + s
                        eng.wait_ge(used, 2 * u + s + 1)
                        if gate is None:
                            eng.tensor_tensor(tile(h, n), G[s][:, :], tile(h, n), ALU.add).then_inc(evac[s], 1)
                        else:
                            eng.scalar_tensor_tensor(tile(h, n), G[s][:, :], col(modc, gate + n), tile(h, n),
                                                     ALU.mult, ALU.add).then_inc(evac[s], 1)
                        split_lo(u + 1, s)
                        if gains is not None:
                            eng.wait_ge(evac[s], u + 1)
                            operand_lo(xh, xl, n, col(vec, gains + n), x_hi, x_lo, x_before + n)
                        if gains2 is not None:
                            operand_lo(x2h, x2l, n, col(vec, gains2 + n), x2_hi, x2_lo, x2_before + n)
                with eng.Fori(u0, u0 + KD // 2 - last) as u:
                    pair(u)
                if last:
                    pair(u0 + KD // 2 - 1)

            def statistic(idx, eps):
                r = idx - (idx > S_MEAN)
                eng.wait_ge(stat, idx + 1)
                eng.tensor_scalar(var4[:, :], O[:, 0:NB], 1.0 / D, eps, ALU.mult, ALU.add).then_inc(var_ready, 1)
                eng.wait_ge(root_ready, r + 1)
                eng.tensor_tensor(tmp[0][:, :].rearrange("p (b t) -> p b t", b=NB),
                                  ident.unsqueeze(1).to_broadcast([P, NB, P]),
                                  root4[:, :].unsqueeze(2).to_broadcast([P, NB, P]), ALU.mult).then_inc(diag_ready, 1)
                eng.wait_ge(spread, r + 1)
                eng.tensor_copy(rstd[:, :], O[:, :]).then_inc(rstd_ready, 1)

            def attention(layer):
                base = PAIRS * layer

                def slot(i, par, gemm=True, attn=True):
                    p = 2 * i + par
                    a, gp = p - 1, p + base

                    def step(j):
                        g = 3 * par + j
                        return U_QKV[layer] + 3 * i + g // 2, g % 2

                    def project(j):
                        u, s = step(j)
                        eng.wait_ge(used, 2 * u + s + 1)
                        if j < 2:
                            wait(eng, qk_lo, 2 * gp)
                        else:
                            wait(eng, v_tr, gp)
                        if j == 0:
                            eng.scalar_tensor_tensor(qkv[j][:, :], G[s][:, :], HD ** -0.5, rstd[:, :], ALU.mult,
                                                     ALU.mult).then_inc(evac[s], 1)
                        else:
                            eng.tensor_tensor(qkv[j][:, :], G[s][:, :], rstd[:, :], ALU.mult).then_inc(evac[s], 1)
                        split_lo(u + 1, s)

                    def scores_a(hh):
                        n = 3 * (2 * a + hh)
                        for c, (lo, hi) in enumerate(CHUNKS):
                            eng.wait_ge(z_ln, n + c + 1)
                            eng.scalar_tensor_tensor(sp[:, lo:hi], Z[c][:, 0:hi - lo], 0.0, ez[:, lo:hi], ALU.max,
                                                     ALU.add).then_inc(sp_ready, 1)
                        for c, (lo, hi) in enumerate(CHUNKS):
                            eng.wait_ge(sp_ready, n + c + 1)
                            eng.tensor_copy(sph[:, lo:hi], sp[:, lo:hi]).then_inc(sp_hi, 1)

                    def maxima_b(hh):
                        n = 2 * a + hh
                        for b in range(NB):
                            o, w = OFF_Q[b], BLK * (b + 1)
                            c = (0, 0, 1, 2)[b]
                            z0 = o - CHUNKS[c][0]
                            wait_apart(eng, z_done, 3 * (2 * (gp - 1) + hh) + c + 1, passed)
                            eng.tensor_tensor_reduce(sp[:, o:o + w], Z[c][:, z0:z0 + w],
                                                     con[:, C_COUNT + o:C_COUNT + o + w], 1.0, -3e38, ALU.add,
                                                     ALU.max, small[:, b:b + 1]).then_inc(zmax, 1)
                        eng.wait_ge(zmax, NB * n + NB)
                        eng.tensor_scalar(small[:, 4:8], small[:, 0:4], -1.0, None, ALU.mult).then_inc(zneg, 1)

                    def inverse_b(hh):
                        n = 2 * a + hh
                        eng.wait_ge(p_exp, NB * n + NB)
                        eng.reciprocal(small[:, 12:16], small[:, 8:12]).then_inc(rden, 1)

                    def copy_b(hh):
                        lo, hi = CHUNKS[1]
                        eng.wait_ge(p_tr, 3 * (2 * a + hh) + 2)
                        eng.tensor_copy(sp[:, lo:hi], Z[1][:, 0:hi - lo]).then_inc(p_cp_d, 1)

                    def rotate(j):
                        eng.wait_ge(perm, 2 * p + j + 1)
                        eng.tensor_tensor(tmp[j][:, :], T[:, :], con[:, C_SIN:C_SIN + SEQ], ALU.mult).then_inc(rot, 1)

                    def out_lo():
                        eng.wait_ge(o_hi, gp)
                        eng.tensor_tensor(tile(yl, a), O[:, :], f32(tile(yh, a)), ALU.subtract).then_inc(o_lo, 1)

                    if layer == 0:
                        if attn:
                            scores_a(0)
                        if gemm:
                            project(0)
                            project(1)
                        if attn:
                            scores_a(1)
                        if gemm:
                            project(2)
                    else:
                        if attn:
                            maxima_b(0)
                            inverse_b(0)
                        if gemm:
                            project(0)
                            rotate(0)
                        if attn:
                            copy_b(0)
                            maxima_b(1)
                            inverse_b(1)
                        if gemm:
                            project(1)
                            rotate(1)
                        if attn:
                            copy_b(1)
                        if gemm:
                            project(2)
                    if attn:
                        out_lo()

                slot(0, 0, attn=False)
                with eng.Fori(0, PAIRS // 2 - 1) as i:
                    slot(i, 1)
                    slot(i + 1, 0)
                slot(PAIRS // 2 - 1, 1)
                slot(PAIRS // 2, 0, gemm=False)

            def ffn(which, last):
                u, f = U_FFN[which], FT * which
                for part, nt in enumerate(PARTS):
                    def hidden(v):
                        n = v - u
                        if which < 2:
                            eng.wait_ge(used, 2 * v + 1)
                            wait(eng, silu, n + f)
                            eng.tensor_tensor(gs[:, :], G[0][:, :], rstd[:, :], ALU.mult).then_inc(evac[0], 1)
                            split_lo(v + 1, 0)
                            eng.wait_ge(used, 2 * v + 2)
                            wait(eng, a_raw, n + f)
                            eng.tensor_tensor(us[:, :], G[1][:, :], rstd[:, :], ALU.mult).then_inc(evac[1], 1)
                            split_lo(v + 1, 1)
                        else:
                            split_lo(v + 1, 0)
                            eng.wait_ge(used, 2 * v + 2)
                            eng.wait_ge(evac[0], v + 1)
                            eng.wait_ge(a_lo, n + f)
                            eng.tensor_tensor(csb[:, :], G[1][:, :], sgt[:, :], ALU.mult).then_inc(evac[1], 1)
                            split_lo(v + 1, 1)
                    loop(eng, u, u + nt, hidden, peel=which + part == 0)
                    u, f = u + nt, f + nt
                    if part < len(PARTS) - 1:
                        residual(u, gate=M_G2 if which == 2 else None)
                    else:
                        last(u)
                    u += KD // 2

            def modulated(gm, shift, hi, lo, before, x_before):
                with eng.Fori(0, KD // 2) as i:
                    for s in range(2):
                        n = 2 * i + s
                        eng.wait_ge(x_lo, n + x_before - 1)
                        eng.scalar_tensor_tensor(tmp[s][:, :], tile(h, n), col(gmc, gm + n), rstd[:, :], ALU.mult,
                                                 ALU.mult).then_inc(mod_t, 1)
                    for s in range(2):
                        n = 2 * i + s
                        eng.wait_ge(x_hi, n + x_before + 1)
                        eng.wait_ge(mod_t, n + before + 1)
                        eng.scalar_tensor_tensor(tile(lo, n), tmp[s][:, :], col(modc, shift + n), f32(tile(hi, n)),
                                                 ALU.add, ALU.subtract).then_inc(x_lo, 1)

            def taps(t, half, part, tile_i):
                ks = list(HALVES[half][0])
                cut = [0, 4, 8, len(ks)]
                for m in range(cut[part], cut[part + 1]):
                    k = ks[m]
                    done_before = ND * tile_i + k
                    src = cin[:, :, k:k + SEQ]
                    weight = col(vec, CONF_K * t + V_CW + k)
                    if k == 0:
                        eng.tensor_scalar(tile(acc, t), tile(src, t), weight, None, ALU.mult).then_inc(tap_d, 1)
                    else:
                        eng.wait_ge(tap_d, done_before)
                        eng.scalar_tensor_tensor(tile(acc, t), tile(src, t), weight, tile(acc, t), ALU.mult,
                                                 ALU.add).then_inc(tap_d, 1)

            def conv_end(t):
                eng.wait_ge(tap_p, NP_OPS * t + NP_OPS)
                eng.wait_ge(tap_d, ND * t + ND)
                eng.scalar_tensor_tensor(tile(acc, t), tile(acc, t), col(vec, V_CB + t), tmp[0][:, :], ALU.add,
                                         ALU.add).then_inc(u_ready, 1)

            for s in range(2):
                split_lo(0, s)
            for n in range(KD):
                operand_lo(xh, xl, n, vec[:, V_MIX0 + n:V_MIX0 + n + 1], x_hi, x_lo, n)
            eng.wait_ge(in_con, 16)
            for dst, c in ((ntri, C_NTRI), (nones, C_NONE), (idb, C_ID), (maskb, C_MASK)):
                eng.tensor_copy(dst[:, :], con[:, c:c + P]).then_inc(consts, 1)
            statistic(S_IN, EPS)
            eng.wait_ge(rstd_ready, 1)
            attention(0)
            residual(U_WO[0], x_before=KD, gains=V_FFN0)
            statistic(S_FFN0, EPS)
            eng.wait_ge(rstd_ready, 2)
            ffn(0, lambda u: residual(u, x_before=2 * KD, gains=V_MIX1, x2_before=0, gains2=V_KV))
            statistic(S_MID, EPS)
            eng.wait_ge(rstd_ready, 3)
            attention(1)
            residual(U_WO[1], x_before=3 * KD, gains=V_FFN1)
            statistic(S_FFN1, EPS)
            eng.wait_ge(rstd_ready, 4)
            ffn(1, lambda u: residual(u))
            eng.wait_ge(ada_mm, 48)
            eng.tensor_tensor(modc[:, :], M[:, 0:48], vec[:, V_ADA:V_ADA + 48], ALU.add).then_inc(modc_ready, 1)
            eng.wait_ge(modc_ready, 1)
            for at, scale, gain in ((0, M_SC1, V_MIX2), (KD, M_SC2, V_FFN2)):
                eng.scalar_tensor_tensor(gmc[:, at:at + KD], modc[:, scale:scale + KD], 1.0, vec[:, gain:gain + KD],
                                         ALU.add, ALU.mult).then_inc(gmc_ready, 1)
            statistic(S_FIN, EPS)
            eng.wait_ge(rstd_ready, 5)
            for n in range(KD):
                eng.scalar_tensor_tensor(h[:, n, :], h[:, n, :], vec[:, V_FIN + n:V_FIN + n + 1], rstd[:, :],
                                         ALU.mult, ALU.mult).then_inc(y_ready, 1)
            statistic(S_MIX2, EPS)
            eng.wait_ge(rstd_ready, 6)
            eng.wait_ge(gmc_ready, 2)
            eng.wait_ge(y_ready, KD)
            modulated(0, M_SH1, xh, xl, 0, 4 * KD)
            eng.wait_ge(padded, 2)
            with eng.Fori(U_CONF, U_CONF + KD) as u:
                eng.wait_ge(evac[1], u + 1)
                eng.tensor_tensor(cin[:, bass.ds(u - U_CONF, 1), PADC:].rearrange("p a s -> p (a s)"), G[0][:, :],
                                  sgt[:, :], ALU.mult).then_inc(evac[0], 1)
                split_lo(u + 1, 0)
                split_lo(u + 1, 1)
            eng.wait_ge(evac[0], U_CONF + KD)

            def short(i):
                for par in range(2):
                    n = 2 * i + par

                    def step(j):
                        g = 3 * par + j
                        return U_SHORT + 3 * i + g // 2, g % 2
                    u, s = step(0)
                    split_lo(u + 1, s)
                    taps(i, par, 0, i)
                    uc, sc = u, s
                    u, s = step(1)
                    eng.wait_ge(evac[sc], uc + 1)
                    eng.wait_ge(used, 2 * u + s + 1)
                    wait(eng, s_lo, n)
                    eng.tensor_tensor(cv[:, PADS:], G[s][:, :], csb[:, :], ALU.mult).then_inc(evac[s], 1)
                    split_lo(u + 1, s)
                    uv, sv = u, s
                    taps(i, par, 1, i)
                    for k in range(SHORT_K):
                        weight = col(vec, SHORT_K * n + V_SW + k)
                        if k == 0:
                            eng.wait_ge(evac[sv], uv + 1)
                            eng.tensor_scalar(sq[1][:, :], cv[:, 0:SEQ], weight, None, ALU.mult).then_inc(s_tap, 1)
                        else:
                            eng.wait_ge(s_tap, SHORT_K * n + k)
                            eng.scalar_tensor_tensor(sq[1][:, :], cv[:, k:k + SEQ], weight, sq[1][:, :], ALU.mult,
                                                     ALU.add).then_inc(s_tap, 1)
                    u, s = step(2)
                    eng.wait_ge(s_tap, SHORT_K * n + SHORT_K)
                    eng.wait_ge(used, 2 * u + s + 1)
                    eng.tensor_tensor(sq[0][:, :], G[s][:, :], sq[1][:, :], ALU.mult).then_inc(evac[s], 1)
                    split_lo(u + 1, s)
                    taps(i, par, 2, i)
                    eng.wait_ge(s_hi, n + 1)
                    eng.wait_ge(evac[s], u + 1)
                    eng.tensor_tensor(tile(yl, n), sq[0][:, :], f32(tile(yh, n)), ALU.subtract).then_inc(s_lo, 1)
                conv_end(i)
            loop(eng, 0, KD // 2, short, peel=True)
            with eng.Fori(0, KD // 2) as i:
                for par in range(2):
                    u = U_GA + 2 * i + par
                    split_lo(u + 1, 0)
                    taps(i + KD // 2, par, 0, i + KD // 2)
                    taps(i + KD // 2, par, 1, i + KD // 2)
                    eng.wait_ge(used, 2 * u + 2)
                    eng.wait_ge(evac[0], u + 1)
                    eng.tensor_tensor(tile(ma, 2 * i + par), G[1][:, :], sgt[:, :], ALU.mult).then_inc(evac[1], 1)
                    split_lo(u + 1, 1)
                    taps(i + KD // 2, par, 2, i + KD // 2)
                conv_end(i + KD // 2)
            eng.wait_ge(stat, S_MEAN + 1)
            eng.tensor_scalar(tmp[0][:, :], O[:, :], 1.0 / D, None, ALU.mult).then_inc(var_ready, 1)
            eng.wait_ge(var_ready, S_MEAN + 1)
            eng.wait_ge(u_ready, KD)
            with eng.Fori(U_GB, U_GB + KD // 2) as u:
                for s in range(2):
                    n = 2 * (u - U_GB) + s
                    eng.tensor_tensor(tile(acc, n), tile(acc, n), tmp[0][:, :], ALU.subtract).then_inc(centred, 1)
                    split_lo(u + 1, s)
            statistic(S_VAR, LN_EPS)
            eng.wait_ge(rstd_ready, 7)
            eng.wait_ge(centred, KD)

            def ln_lo(n):
                eng.wait_ge(u_hi, n + 1)
                eng.tensor_tensor(yl[:, n, :], acc[:, n, :], f32(yh[:, n, :]), ALU.subtract).then_inc(u_lo, 1)

            for n in range(KD):
                eng.tensor_tensor(acc[:, n, :], acc[:, n, :], rstd[:, :], ALU.mult).then_inc(ln_t, 1)
                if n >= 2:
                    ln_lo(n - 2)
            ln_lo(KD - 2)
            ln_lo(KD - 1)
            eng.wait_ge(evac[1], U_GB)

            def mix(u):
                for s in range(2):
                    n = 2 * (u - U_CO) + s
                    wait(eng, mix_lo, n - 1)
                    eng.wait_ge(used, 2 * u + s + 1)
                    eng.tensor_tensor(tmp[s][:, :], G[s][:, :], tile(sgb, n), ALU.mult).then_inc(evac[s], 1)
                    split_lo(u + 1, s)
                    eng.wait_ge(evac[s], u + 1)
                    eng.tensor_tensor(tmp[s][:, :], tmp[s][:, :], tile(ma, n), ALU.add).then_inc(mix_t, 1)
                    eng.wait_ge(mix_hi, n + 1)
                    eng.tensor_tensor(tile(xl, n), tmp[s][:, :], f32(tile(xh, n)), ALU.subtract).then_inc(mix_lo, 1)
            loop(eng, U_CO, U_CO + KD // 2, mix, peel=True)
            residual(U_OUT, gate=M_G1)
            statistic(S_FFN2, EPS)
            eng.wait_ge(rstd_ready, 8)
            modulated(KD, M_SH2, yh, yl, KD, 5 * KD)
            ffn(2, lambda u: residual(u, gate=M_G2, last=True))
            statistic(S_OUT, EPS)
            eng.wait_ge(rstd_ready, 9)
            for n in range(KD):
                eng.scalar_tensor_tensor(h[:, n, :], h[:, n, :], vec[:, V_FIN2 + n:V_FIN2 + n + 1], rstd[:, :],
                                         ALU.mult, ALU.mult).then_inc(done, 1)

        @block.gpsimd
        def _(eng):
            def clear(count):
                eng.memset(ssum[:, :], 0.0).then_inc(ss_clear, 1)
                eng.wait_ge(ss_clear, count + 1)

            def add_square(s, count):
                eng.wait_ge(sq_ready, count + 1)
                wait(eng, sq_added, count)
                eng.tensor_tensor(ssum[:, :], ssum[:, :], sq[s][:, :], ALU.add).then_inc(sq_added, 1)

            def add_round(rnd):
                with eng.Fori(0, KD // 2) as i:
                    for s in range(2):
                        add_square(s, 2 * i + s + 8 * rnd)

            def inverse_root(idx, cleared):
                eng.wait_ge(var_ready, idx + 1)
                eng.tensor_tensor(root4[:, :], var4[:, :], mhalf[:, 0:1].to_broadcast([P, NB]), ALU.pow)\
                   .then_inc(root_ready, 1)
                clear(cleared)

            def attention(layer):
                base = PAIRS * layer

                def slot(i, par, gemm=True, attn=True):
                    p = 2 * i + par
                    a, gp = p - 1, p + base

                    def lo(dst_h, dst_l, j):
                        eng.wait_ge(qk_hi, 2 * gp + j + 1)
                        eng.tensor_tensor(dst_l[par][:, :], qkv[j][:, :], f32(dst_h[par][:, :]),
                                          ALU.subtract).then_inc(qk_lo, 1)

                    def scores_a(hh):
                        for c, (x, y) in enumerate(CHUNKS):
                            eng.wait_ge(sp_hi, 3 * (2 * a + hh) + c + 1)
                            eng.tensor_tensor(spl[:, x:y], sp[:, x:y], f32(sph[:, x:y]), ALU.subtract).then_inc(sp_lo, 1)

                    def normalise_b(hh):
                        wait_apart(eng, rden, 2 * a + hh + 1, passed)
                        for b in range(NB):
                            o, w = OFF_Q[b], BLK * (b + 1)
                            eng.tensor_scalar(ez[:, o:o + w], ez[:, o:o + w], small[:, 12 + b:13 + b], None,
                                              ALU.mult).then_inc(p_norm, 1)

                    def rotate(j):
                        eng.wait_ge(rot, 2 * p + j + 1)
                        eng.tensor_tensor(qkv[j][:, :], qkv[j][:, :], con[:, C_COS:C_COS + SEQ],
                                          ALU.mult).then_inc(roped_c, 1)
                        eng.wait_ge(roped_c, 2 * p + j + 1)
                        eng.tensor_tensor(qkv[j][:, :], qkv[j][:, :], tmp[j][:, :], ALU.add).then_inc(roped, 1)

                    if layer == 0:
                        if attn:
                            scores_a(0)
                        if gemm:
                            lo(qh, ql, 0)
                        if attn:
                            scores_a(1)
                        if gemm:
                            lo(kh, kl, 1)
                    else:
                        if attn:
                            normalise_b(0)
                        if gemm:
                            rotate(0)
                            lo(qh, ql, 0)
                        if attn:
                            normalise_b(1)
                        if gemm:
                            rotate(1)
                            lo(kh, kl, 1)

                slot(0, 0, attn=False)
                with eng.Fori(0, PAIRS // 2 - 1) as i:
                    slot(i, 1)
                    slot(i + 1, 0)
                slot(PAIRS // 2 - 1, 1)
                slot(PAIRS // 2, 0, gemm=False)

            def fold_ada(which, part, rnd=None):
                def pair(idx):
                    for s in range(2):
                        j = 2 * idx + s
                        eng.wait_ge(ada_land[s], 16 * (idx + 1))
                        wait(eng, ada_sum, j)
                        eng.tensor_tensor(aprod[:, :, :], araw[s][:, :, :],
                                          cs[:, :].unsqueeze(2).to_broadcast([P, KD, P]), ALU.mult).then_inc(ada_fold, 1)
                        for m, half in enumerate((4, 2)):
                            eng.wait_ge(ada_fold, 3 * j + m + 1)
                            eng.tensor_tensor(aprod[:, 0:half, :], aprod[:, 0:half, :], aprod[:, half:2 * half, :],
                                              ALU.add).then_inc(ada_fold, 1)
                        eng.wait_ge(ada_fold, 3 * j + 3)
                        wait(eng, ada_mm, j - 1)
                        eng.tensor_tensor(asum[s][:, :], aprod[:, 0, :], aprod[:, 1, :], ALU.add).then_inc(ada_sum, 1)
                    if rnd is not None:
                        for s in range(2):
                            add_square(s, 2 * (idx - first) + s + 8 * rnd)
                first = 12 * which + 4 * part
                loop(eng, first, first + KD // 2, pair, peel=first == 0)

            def ffn(which, hid_h, hid_l, rnd):
                f = FT * which
                for part, nt in enumerate(PARTS):
                    def hidden(m):
                        n = m - f
                        if which < 2:
                            u = U_FFN[which] + sum(PARTS[:part]) + part * (KD // 2)
                            eng.wait_ge(silu, m + 1)
                            eng.wait_ge(evac[1], u + n + 1)
                            wait(eng, a_lo, m)
                            eng.tensor_tensor(af[:, :], si[:, :], us[:, :], ALU.mult).then_inc(a_raw, 1)
                            eng.wait_ge(a_hi, m + 1)
                            eng.tensor_tensor(tile(hid_l, n), af[:, :], f32(tile(hid_h, n)), ALU.subtract)\
                               .then_inc(a_lo, 1)
                        else:
                            eng.wait_ge(a_hi, m + 1)
                            eng.tensor_tensor(tile(hid_l, n), csb[:, :], f32(tile(hid_h, n)), ALU.subtract)\
                               .then_inc(a_lo, 1)
                    loop(eng, f, f + nt, hidden, peel=f == 0)
                    f += nt
                    if which < 2:
                        fold_ada(which, part, rnd if part == len(PARTS) - 1 else None)
                if which == 2:
                    add_round(rnd)

            def taps(t, half):
                for k in HALVES[half][1]:
                    m = k - ND
                    src = tile(cin[:, :, k:k + SEQ], t)
                    weight = col(vec, CONF_K * t + V_CW + k).to_broadcast([P, SEQ])
                    if m == 0:
                        wait(eng, u_ready, t)
                        eng.tensor_tensor(tmp[0][:, :], src, weight, ALU.mult).then_inc(tap_p, 1)
                    else:
                        before = NP_OPS * t + 2 * m - 1
                        eng.wait_ge(tap_p, before)
                        eng.tensor_tensor(tmp[1][:, :], src, weight, ALU.mult).then_inc(tap_p, 1)
                        eng.wait_ge(tap_p, before + 1)
                        eng.tensor_tensor(tmp[0][:, :], tmp[0][:, :], tmp[1][:, :], ALU.add).then_inc(tap_p, 1)

            def add_u(t):
                eng.wait_ge(u_ready, t + 1)
                wait(eng, u_added, t)
                eng.tensor_tensor(ssum[:, :], ssum[:, :], tile(acc, t), ALU.add).then_inc(u_added, 1)

            eng.memset(mhalf[:, :], -0.5).then_inc(ss_clear, 1)
            clear(1)
            for n in range(KD):
                add_square(n % 2, n)
            inverse_root(S_IN, 2)
            attention(0)
            add_round(Q_FFN0)
            inverse_root(S_FFN0, 3)
            eng.wait_ge(cs_ready, 1)
            ffn(0, yh, yl, Q_MID)
            inverse_root(S_MID, 4)
            attention(1)
            add_round(Q_FFN1)
            inverse_root(S_FFN1, 5)
            ffn(1, yh, yl, Q_FIN)
            inverse_root(S_FIN, 6)
            eng.memset(cin[:, :, 0:PADC], 0.0).then_inc(padded, 1)
            eng.memset(cv[:, 0:PADS], 0.0).then_inc(padded, 1)
            for n in range(KD):
                add_square(n % 2, n + 8 * Q_MIX2)
            inverse_root(S_MIX2, 7)
            eng.wait_ge(evac[0], U_CONF + KD)

            def conv(t):
                taps(t, 0)
                taps(t, 1)
                add_u(t)
            loop(eng, 0, KD, conv, peel=True)
            eng.wait_ge(var_ready, S_MEAN + 1)
            clear(8)
            add_round(Q_VAR)
            inverse_root(S_VAR, 9)
            add_round(Q_FFN2)
            inverse_root(S_FFN2, 10)
            ffn(2, xh, xl, Q_OUT)
            inverse_root(S_OUT, 11)

        @block.tensor
        def _(eng):
            def product(u, s, src_h, src_l, ready, before, kt=KD, ks=None):
                for k in (range(kt) if ks is None else ks):
                    if k == 0:
                        eng.wait_ge(w_lo, 2 * u + s + 1)
                        wait(eng, evac[s], u)
                    eng.wait_ge(ready, before + k + 1)
                    eng.matmul(G[s][:, :], wh[s][:, k, :], src_h[:, k, :], start=k == 0, stop=False)
                    eng.matmul(G[s][:, :], wh[s][:, k, :], src_l[:, k, :], start=False, stop=False)
                    mm = eng.matmul(G[s][:, :], wl[s][:, k, :], src_h[:, k, :], start=False, stop=k == kt - 1)
                    if k == kt - 1:
                        mm.then_inc(used, 1)

            def steps(u0, pairs, src_h, src_l, ready, before, kt=KD):
                with eng.Fori(u0, u0 + pairs) as u:
                    for s in range(2):
                        product(u, s, src_h, src_l, ready, before, kt)

            def statistic(ready, count):
                eng.wait_ge(ready, count)
                for b in range(NB):
                    mm = eng.matmul(O[:, b:b + 1], ssum[:, BLK * b:BLK * b + BLK], ones[:, 0:1], start=True, stop=True)
                mm.then_inc(stat, 1)

            def spread_root(idx):
                eng.wait_ge(diag_ready, idx - (idx > S_MEAN) + 1)
                eng.matmul(O[:, :], ones, tmp[0][:, :], start=True, stop=True).then_inc(spread, 1)

            def attention(layer):
                base = PAIRS * layer
                x_before = 2 * KD * layer

                def slot(i, par, gemm=True, attn=True):
                    p = 2 * i + par
                    a, gp, ap = p - 1, p + base, 1 - par

                    def step(j):
                        g = 3 * par + j
                        return U_QKV[layer] + 3 * i + g // 2, g % 2

                    def project(lo, hi):
                        if not gemm:
                            return
                        for j in range(3):
                            ks = range(max(lo - 8 * j, 0), min(hi - 8 * j, 8))
                            u, s = step(j)
                            if len(ks) == 0:
                                continue
                            if layer == 1 and j > 0:
                                product(u, s, x2h, x2l, x2_lo, 0, ks=ks)
                            else:
                                product(u, s, xh, xl, x_lo, x_before, ks=ks)

                    def scores(hh):
                        rows = slice(HD * hh, HD * hh + HD)
                        if hh == 0:
                            eng.wait_ge(qk_lo, 2 * gp)
                        for c in range(3):
                            strips = {0: (3, 2), 1: (1,), 2: (0,)}[c] if layer == 0 else {0: (0, 1), 1: (2,), 2: (3,)}[c]
                            for m, b in enumerate(strips):
                                blk = slice(BLK * b, BLK * b + BLK)
                                if layer == 0:
                                    o = OFF_K[b] - CHUNKS[c][0]
                                    w = SEQ - BLK * b
                                    out = Z[c][:, o:o + w]
                                    st, mv = (kh[ap], kl[ap]), (qh[ap], ql[ap])
                                    cols = slice(BLK * b, SEQ)
                                else:
                                    o = OFF_Q[b] - CHUNKS[c][0]
                                    w = BLK * (b + 1)
                                    out = Z[c][:, o:o + w]
                                    st, mv = (qh[ap], ql[ap]), (kh[ap], kl[ap])
                                    cols = slice(0, w)
                                for x, y in ((0, 0), (0, 1), (1, 0)):
                                    mm = eng.matmul(out, st[x][rows, blk], mv[y][rows, cols],
                                                    start=(m == 0 and x == 0 and y == 0), stop=False,
                                                    skip_group_check=True)
                                if layer == 0:
                                    mm = eng.matmul(out[:, 0:BLK], idb[:, :], maskb[:, :], start=False, stop=False,
                                                    skip_group_check=True)
                            mm.then_inc(z_done, 1)

                    def cumulate(hh):
                        n = 3 * (2 * a + hh)
                        for c, strips in enumerate(((3, 2), (1,), (0,))):
                            eng.wait_ge(sp_lo, n + c + 1)
                            for b in strips:
                                o = OFF_K[b] - CHUNKS[c][0]
                                for later in range(b, NB):
                                    w = SEQ - BLK * later
                                    at = o + BLK * (later - b)
                                    for part in (sph, spl):
                                        mm = eng.matmul(Z[c][:, at:at + w], (ntri if later == b else nones)[:, :],
                                                        part[:, OFF_K[later]:OFF_K[later] + w], start=False,
                                                        stop=False, skip_group_check=True)
                            mm.then_inc(cum, 1)

                    def transpose_b(hh):
                        eng.wait_ge(p_norm, NB * (2 * a + hh) + NB)
                        for c, strips in enumerate(((3, 2), (1,), (0,))):
                            for b in strips:
                                for q in range(b, NB):
                                    o = OFF_K[b] - CHUNKS[c][0] + BLK * (q - b)
                                    at = OFF_Q[q] + BLK * b
                                    mm = eng.transpose(Z[c][:, o:o + BLK], ez[:, at:at + BLK], ident)
                            mm.then_inc(p_tr, 1)

                    def weighted(hh):
                        rows = slice(HD * hh, HD * hh + HD)
                        n = 2 * a + hh
                        if hh == 0:
                            eng.wait_ge(v_nat, gp)
                        for b in (3, 2, 1, 0):
                            if layer == 0:
                                eng.wait_ge(w_exp, 3 * n + (3, 2, 1, 1)[b])
                            elif b == 1:
                                eng.wait_ge(p_cp_d, n + 1)
                            else:
                                eng.wait_ge(p_cp_a, 2 * n + (2, 0, 1, 1)[b])
                            w = SEQ - BLK * b
                            src = (wa if layer == 0 else sp)[:, OFF_K[b]:OFF_K[b] + w]
                            mm = eng.matmul(O[rows, BLK * b:SEQ], vn[ap][:, b, rows], src, start=b == 3, stop=b == 0,
                                            skip_group_check=True)
                        mm.then_inc(pv_done, 1)

                    def values():
                        u, s = step(-1)
                        eng.wait_ge(evac[s], u + 1)
                        if layer == 1:
                            eng.wait_ge(rot, 2 * p)
                        for b in range(NB):
                            mm = eng.transpose(T[:, BLK * b:BLK * b + BLK], qkv[2][:, BLK * b:BLK * b + BLK], ident)
                        mm.then_inc(v_tr, 1)

                    def swap(j):
                        u, s = step(j)
                        eng.wait_ge(evac[s], u + 1)
                        if j == 0:
                            wait(eng, v_nat, gp)
                        else:
                            eng.wait_ge(rot, 2 * p + 1)
                        eng.matmul(T[:, :], con[:, C_PERM:C_PERM + P], qkv[j][:, :], start=True, stop=True)\
                           .then_inc(perm, 1)

                    if layer == 0:
                        if attn:
                            scores(0)
                        project(0, 8)
                        if not attn:
                            statistic(sq_added, KD)
                        if attn:
                            cumulate(0)
                            values()
                        project(8, 12)
                        if not attn:
                            spread_root(S_IN)
                        if attn:
                            weighted(0)
                            scores(1)
                        project(12, 20)
                        if attn:
                            cumulate(1)
                        project(20, 24)
                        if attn:
                            weighted(1)
                    else:
                        project(0, 4)
                        if attn:
                            scores(0)
                            values()
                        project(4, 8)
                        if not attn:
                            statistic(sq_added, KD * (Q_MID + 1))
                        project(8, 10)
                        if not attn:
                            spread_root(S_MID)
                        if attn:
                            transpose_b(0)
                        if gemm:
                            swap(0)
                        project(10, 14)
                        if attn:
                            weighted(0)
                            scores(1)
                        project(14, 20)
                        if attn:
                            transpose_b(1)
                        if gemm:
                            swap(1)
                        project(20, 24)
                        if attn:
                            weighted(1)

                slot(0, 0, attn=False)
                with eng.Fori(0, PAIRS // 2 - 1) as i:
                    slot(i, 1)
                    slot(i + 1, 0)
                slot(PAIRS // 2 - 1, 1)
                slot(PAIRS // 2, 0, gemm=False)

            def ffn(which, src_h, src_l, hid_h, hid_l, x_before, stat_idx=None, count=None):
                u, f = U_FFN[which], FT * which
                for part, nt in enumerate(PARTS):
                    if part == 0 and stat_idx is not None:
                        product(u, 0, src_h, src_l, x_lo, x_before)
                        statistic(sq_added, count)
                        product(u, 1, src_h, src_l, x_lo, x_before, ks=range(0, 3))
                        spread_root(stat_idx)
                        product(u, 1, src_h, src_l, x_lo, x_before, ks=range(3, KD))
                        steps(u + 1, nt - 1, src_h, src_l, x_lo, x_before)
                    else:
                        steps(u, nt, src_h, src_l, x_lo, x_before)
                    u += nt
                    with eng.Fori(u, u + KD // 2) as v:
                        for s in range(2):
                            product(v, s, hid_h, hid_l, a_lo, f, nt)
                            if which < 2:
                                j = 2 * (v + (12 * which + 4 * part - u)) + s
                                eng.wait_ge(ada_sum, j + 1)
                                eng.matmul(col(M, j), asum[s][:, :], ones[:, 0:1], start=True, stop=True)\
                                   .then_inc(ada_mm, 1)
                    u, f = u + KD // 2, f + nt

            eng.wait_ge(in_con, 16)
            eng.wait_ge(consts, 4)
            attention(0)
            steps(U_WO[0], 4, yh, yl, o_lo, 0)
            ffn(0, xh, xl, yh, yl, KD, S_FFN0, KD * (Q_FFN0 + 1))
            attention(1)
            steps(U_WO[1], 4, yh, yl, o_lo, PAIRS)
            ffn(1, xh, xl, yh, yl, 3 * KD, S_FFN1, KD * (Q_FFN1 + 1))
            statistic(sq_added, KD * (Q_FIN + 1))
            spread_root(S_FIN)
            statistic(sq_added, KD * (Q_MIX2 + 1))
            spread_root(S_MIX2)
            steps(U_CONF, 8 + 12, xh, xl, x_lo, 4 * KD)
            with eng.Fori(U_GA, U_GA + KD) as u:
                product(u, 0, xh, xl, x_lo, 4 * KD)
                product(u, 1, yh, yl, s_lo, 0)
            eng.wait_ge(u_added, KD)
            eng.matmul(O[:, :], ones, ssum[:, :], start=True, stop=True).then_inc(stat, 1)
            steps(U_GB, 4, xh, xl, x_lo, 4 * KD)
            statistic(sq_added, KD * (Q_VAR + 1))
            spread_root(S_VAR)
            steps(U_CO, 4, yh, yl, u_lo, 0)
            steps(U_OUT, 4, xh, xl, mix_lo, 0)
            statistic(sq_added, KD * (Q_FFN2 + 1))
            spread_root(S_FFN2)
            ffn(2, yh, yl, xh, xl, 5 * KD)
            statistic(sq_added, KD * (Q_OUT + 1))
            spread_root(S_OUT)


def tiles(w):
    k, n = w.shape
    return w.reshape(k // P, P, n // P, P).transpose(2, 1, 0, 3)


def ffn_tiles(gate, up, down):
    g, u, at = tiles(gate), tiles(up), 0
    out = []
    for nt in PARTS:
        out.append(np.stack([g[at:at + nt], u[at:at + nt]], 1).reshape(2 * nt, P, KD, P))
        d = np.zeros((KD, P, KD, P), down.dtype)
        d[:, :, 0:nt] = tiles(down[at * P:(at + nt) * P])
        out.append(d)
        at += nt
    return out


def columns(v):
    return v.reshape(-1, P).T


def kernel(**inp):
    import concourse.bacc as bacc
    from concourse.bass_utils import run_bass_kernel_spmd

    a = {k: np.asarray(v) for k, v in inp.items()}
    turn = lambda *ts: np.stack(ts, 1).reshape(-1, P, KD, P)
    qkv_a, kv = tiles(a["w_qkv_a"][0]), tiles(a["w_kv"])
    w_in = tiles(a["w_in_2"][0])
    b_s, c_s, v_s, v_c, gl_c, g_a, g_b = [w_in[KD * i:KD * i + KD] for i in range(7)]
    stream = np.concatenate(
        [turn(qkv_a[0:8], qkv_a[8:16], qkv_a[16:24]), tiles(a["w_o_a"][0])]
        + ffn_tiles(a["w_gate"][0], a["w_up"][0], a["w_down"][0])
        + [turn(tiles(a["w_q_b"][0]), kv[0:8], kv[8:16]), tiles(a["w_o_b"][0])]
        + ffn_tiles(a["w_gate"][1], a["w_up"][1], a["w_down"][1])
        + [turn(v_c, gl_c), turn(c_s, v_s, b_s), turn(g_a, tiles(a["w_short_out_2"][0])), g_b,
           tiles(a["w_conf_out_2"][0]), tiles(a["w_o_2"][0])]
        + ffn_tiles(a["w_ffn_in_2"][0][:, :DFF], a["w_ffn_in_2"][0][:, DFF:], a["w_ffn_out_2"][0]))
    assert stream.shape[0] == 2 * U_END
    vectors = np.concatenate(
        [columns(v) for v in (
            a["norm_mix"][0], a["norm_mix"][1], a["norm_kv"], a["norm_ffn"][0], a["norm_ffn"][1], a["norm_final"],
            a["norm_mix_g_2"][0], a["conv_conf_b_2"][0], a["conf_ln_g_2"][0], a["conf_ln_b_2"][0],
            a["norm_ffn_g_2"][0], a["final_norm_g_2"], a["c_2"][0], a["b_ada_2"][0])]
        + [w.reshape(k, KD, P).transpose(2, 1, 0).reshape(P, KD * k)
           for w, k in ((a["conv_short_w_2"][0], SHORT_K), (a["conv_conf_w_2"][0], CONF_K))], 1)
    arrays = {
        "x_t": a["x"][0].T.reshape(KD, P, SEQ).transpose(1, 0, 2),
        "const_d": constants(),
        "vec_d": vectors,
        "stream": stream,
        "ada_w": tiles(a["w_ada_2"][0]),
    }
    arrays = {k: np.ascontiguousarray(v) for k, v in arrays.items()}
    nc = bacc.Bacc("TRN2", target_bir_lowering=False, num_devices=1)
    args = [nc.dram_tensor(k, list(v.shape), F32, kind="ExternalInput").ap() for k, v in arrays.items()]
    args.append(nc.dram_tensor("out_t", [P, KD, SEQ], F32, kind="ExternalOutput").ap())
    build_program(nc, *args)
    got = run_bass_kernel_spmd(nc, [arrays], core_ids=[0]).results[0]["out_t"]
    return got.transpose(1, 0, 2).reshape(D, SEQ).T.reshape(1, SEQ, D)
```

```python
from contextlib import ExitStack

import numpy as np

import concourse.bass as bass
from concourse import mybir

F32 = mybir.dt.float32
F32R = mybir.dt.float32r
BF16 = mybir.dt.bfloat16
ALU = mybir.AluOpType
ACT = mybir.ActivationFunctionType

P = 128
SEQ = 512
D = 1024
KD = D // P
HEADS = 16
HD = 64
PAIRS = HEADS // 2
DFF = 2816
FT = DFF // P
PARTS = (8, 8, 6)
SHORT_K = 3
CONF_K = 31
EPS = 1e-6
LN_EPS = 1e-5
BLK = 128
NB = SEQ // BLK
NEG = -1e30

U_QKV = (0, 50)
U_WO = (12, 62)
U_FFN = (16, 66, 140)
U_CONF, U_SHORT, U_GA, U_GB, U_CO, U_OUT = 100, 108, 120, 128, 132, 136
ADA_TILES = PARTS[0] + KD + PARTS[1]
assert ADA_TILES * 2 == 48
U_END = U_FFN[2] + (2 * FT + len(PARTS) * KD) // 2

CHUNKS = ((0, 384), (384, 768), (768, 1280))
OFF_K = {3: 0, 2: 128, 1: 384, 0: 768}
OFF_Q = {0: 0, 1: 128, 2: 384, 3: 768}
TRI = 1280

C_ID, C_ONE, C_NTRI, C_NONE, C_MASK, C_PERM, C_COS, C_SIN, C_COUNT = 0, 128, 256, 384, 512, 640, 768, 1280, 1792
C_ALL = C_COUNT + TRI
V_MIX0, V_MIX1, V_KV, V_FFN0, V_FFN1, V_FIN, V_MIX2, V_CB, V_LG, V_LB, V_FFN2, V_FIN2, V_C, V_ADA = (
    0, 8, 16, 24, 32, 40, 48, 56, 64, 72, 80, 88, 96, 104)
V_SW = V_ADA + 48
V_CW = V_SW + KD * SHORT_K
V_ALL = V_CW + KD * CONF_K
M_SH1, M_SC1, M_G1, M_SH2, M_SC2, M_G2 = 0, 8, 16, 24, 32, 40

ND = 21
NV_OPS = ND + 1
NP_OPS = 2 * (CONF_K - ND) - 1


def constants():
    t = np.zeros((P, C_ALL), np.float32)
    i, j = np.arange(P)[:, None], np.arange(P)[None, :]
    t[:, C_ID:C_ID + P] = i == j
    t[:, C_ONE:C_ONE + P] = 1.0
    t[:, C_NTRI:C_NTRI + P] = -(i >= j).astype(np.float32)
    t[:, C_NONE:C_NONE + P] = -1.0
    t[:, C_MASK:C_MASK + P] = np.where(i < j, 0.0, NEG)
    half = HD // 2
    for m in range(P):
        head, r = divmod(m, HD)
        if r < half:
            t[head * HD + r + half, C_PERM + m] = -1.0
        else:
            t[head * HD + r - half, C_PERM + m] = 1.0
    freq = (np.float32(10000.0) ** (-np.arange(0, HD, 2, dtype=np.float32) / np.float32(HD))).astype(np.float32)
    angle = (np.arange(SEQ, dtype=np.float32)[None, :] * freq[:, None]).astype(np.float32)
    t[:, C_COS:C_COS + SEQ] = np.tile(np.cos(angle), (4, 1))
    t[:, C_SIN:C_SIN + SEQ] = np.tile(np.sin(angle), (4, 1))
    for b in range(NB):
        q = b * BLK + np.arange(P)[:, None]
        k = np.arange(BLK * (b + 1))[None, :]
        dist = q - k
        n = (((dist >= 0) & (dist <= 128)).astype(np.int64)
             + ((dist >= 0) & (dist % 4 == 0)) + ((dist >= 0) & (dist % 16 == 0)))
        t[:, C_COUNT + OFF_Q[b]:C_COUNT + OFF_Q[b] + BLK * (b + 1)] = np.where(
            n > 0, np.log(np.maximum(n, 1).astype(np.float64)), NEG)
    return t


def wait(eng, sem, value):
    if isinstance(value, int) and value <= 0:
        return
    eng.wait_ge(sem, value)


def wait_apart(eng, sem, value, passed):
    eng.wait_ge(sem, value)
    if not isinstance(value, int):
        eng.sem_inc(passed, 1)


def loop(eng, lo, hi, body, peel=False):
    if peel:
        body(lo)
        lo += 1
    with eng.Fori(lo, hi) as i:
        body(i)


def build_program(nc, x_t, const_d, vec_d, stream, ada_w, out_t):
    with ExitStack() as ctx:
        def sb(name, shape, dt=F32, stack=ctx):
            return stack.enter_context(nc.sbuf_tensor(name, shape, dt))

        def sem(name):
            return ctx.enter_context(nc.semaphore(name))

        h = sb("h", [P, KD, SEQ])
        xh, xl = sb("xh", [P, KD, SEQ], F32R), sb("xl", [P, KD, SEQ], F32R)
        yh, yl = sb("yh", [P, KD, SEQ], F32R), sb("yl", [P, KD, SEQ], F32R)
        raw = [sb(f"raw{s}", [P, KD, P]) for s in range(2)]
        wh = [sb(f"wh{s}", [P, KD, P], F32R) for s in range(2)]
        wl = [sb(f"wl{s}", [P, KD, P], F32R) for s in range(2)]
        con = sb("con", [P, C_ALL])
        vec = sb("vec", [P, V_ALL])
        ntri, nones = sb("ntri", [P, P], F32R), sb("nones", [P, P], F32R)
        idb, maskb = sb("idb", [P, P], BF16), sb("maskb", [P, P], BF16)
        rstd = sb("rstd", [P, SEQ])
        ssum = sb("ssum", [P, SEQ])
        sq = [sb(f"sq{s}", [P, SEQ]) for s in range(2)]
        tmp = [sb(f"tmp{s}", [P, SEQ]) for s in range(2)]
        modc = sb("modc", [P, 48])
        cs = sb("cs", [P, KD])
        small = sb("small", [P, 16])
        var4, root4 = sb("var4", [P, NB]), sb("root4", [P, NB])
        mean4 = sb("mean4", [P, NB])
        gmc = sb("gmc", [P, 16])
        mhalf = sb("mhalf", [P, 1])

        with ExitStack() as r:
            sph, spl, wa = sb("sph", [P, TRI], F32R, r), sb("spl", [P, TRI], F32R, r), sb("wa", [P, TRI], F32, r)
        with ExitStack() as r:
            ma, sgb = sb("ma", [P, KD, SEQ], F32, r), sb("sgb", [P, KD, SEQ], F32, r)
        x2h, x2l = sb("x2h", [P, KD, SEQ], F32R), sb("x2l", [P, KD, SEQ], F32R)

        with ExitStack() as r:
            qh = [sb(f"qh{i}", [P, SEQ], F32R, r) for i in range(2)]
            ql = [sb(f"ql{i}", [P, SEQ], F32R, r) for i in range(2)]
            kh = [sb(f"kh{i}", [P, SEQ], F32R, r) for i in range(2)]
            kl = [sb(f"kl{i}", [P, SEQ], F32R, r) for i in range(2)]
            qkv = [sb(f"qkv{i}", [P, SEQ], F32, r) for i in range(3)]
            vn = [sb(f"vn{i}", [P, NB, P], F32, r) for i in range(2)]
            ez, sp = sb("ez", [P, TRI], F32, r), sb("sp", [P, TRI], F32, r)
        with ExitStack() as r:
            gs, us, si, af = [sb(n, [P, SEQ], F32, r) for n in ("gs", "us", "si", "af")]
            araw = [sb(f"araw{s}", [P, KD, P], F32, r) for s in range(2)]
            aprod = sb("aprod", [P, KD, P], F32, r)
            asum = [sb(f"asum{s}", [P, P], F32, r) for s in range(2)]
        PADC = CONF_K - 1
        PADS = SHORT_K - 1
        cin = sb("cin", [P, KD, PADC + SEQ])
        acc = sb("acc", [P, KD, SEQ])
        csb, sgt = sb("csb", [P, SEQ]), sb("sgt", [P, SEQ])
        cv = sb("cv", [P, PADS + SEQ])

        G = [ctx.enter_context(nc.psum_tensor(f"G{s}", [P, SEQ], F32)) for s in range(2)]
        Z = [ctx.enter_context(nc.psum_tensor(f"Z{s}", [P, SEQ], F32)) for s in range(3)]
        O = ctx.enter_context(nc.psum_tensor("O", [P, SEQ], F32))
        T = ctx.enter_context(nc.psum_tensor("T", [P, SEQ], F32))
        M = ctx.enter_context(nc.psum_tensor("M", [P, SEQ], F32))

        in_vec, in_con = sem("in_vec"), sem("in_con")
        in_h = [sem(f"in_h{n}") for n in range(KD)]
        landed = [sem("landed0"), sem("landed1")]
        w_hi, w_lo = sem("w_hi"), sem("w_lo")
        used = sem("used")
        evac = [sem("evac0"), sem("evac1")]
        consts = sem("consts")
        cs_ready = sem("cs_ready")
        ss_clear = sem("ss_clear")
        sq_ready, sq_added = sem("sq_ready"), sem("sq_added")
        sq2_ready, sq2_added = sem("sq2_ready"), sem("sq2_added")
        sum2_ready = sem("sum2_ready")
        stat = sem("stat")
        var_ready, root_ready = sem("var_ready"), sem("root_ready")
        diag_ready, spread = sem("diag_ready"), sem("spread")
        rstd_ready = sem("rstd_ready")
        mod_t = sem("mod_t")
        x_hi, x_lo = sem("x_hi"), sem("x_lo")
        x2_hi, x2_lo = sem("x2_hi"), sem("x2_lo")
        z_done, z_abs, z_exp, z_ln = sem("z_done"), sem("z_abs"), sem("z_exp"), sem("z_ln")
        sp_ready, sp_hi, sp_lo, cum = sem("sp_ready"), sem("sp_hi"), sem("sp_lo"), sem("cum")
        w_exp = sem("w_exp")
        pv_done = sem("pv_done")
        qk_hi, qk_lo = sem("qk_hi"), sem("qk_lo")
        v_tr, v_nat = sem("v_tr"), sem("v_nat")
        perm, rot = sem("perm"), sem("rot")
        roped_c, roped = sem("roped_c"), sem("roped")
        o_hi, o_lo = sem("o_hi"), sem("o_lo")
        zmax, zneg, p_exp, rden = sem("zmax"), sem("zneg"), sem("p_exp"), sem("rden")
        den_diag, p_tr = sem("den_diag"), sem("p_tr")
        p_cp_a, p_cp_d = sem("p_cp_a"), sem("p_cp_d")
        silu, a_raw, a_hi, a_lo = sem("silu"), sem("a_raw"), sem("a_hi"), sem("a_lo")
        ada_land = [sem("ada_land0"), sem("ada_land1")]
        ada_fold, ada_sum, ada_mm = sem("ada_fold"), sem("ada_sum"), sem("ada_mm")
        modc_ready, gmc_ready, y_ready = sem("modc_ready"), sem("gmc_ready"), sem("y_ready")
        padded = sem("padded")
        tap_d, tap_p = sem("tap_d"), sem("tap_p")
        u_ready, u_added = sem("u_ready"), sem("u_added")
        s_tap = sem("s_tap")
        s_hi, s_lo = sem("s_hi"), sem("s_lo")
        centred, ln_t, ln_s, u_hi, u_lo = [sem(n) for n in ("centred", "ln_t", "ln_s", "u_hi", "u_lo")]
        mix_t, mix_hi, mix_lo = sem("mix_t"), sem("mix_hi"), sem("mix_lo")
        done, stored = sem("done"), sem("stored")
        passed = sem("passed")

        block = ctx.enter_context(nc.Block())

        def f32(ap):
            return ap.bitcast(F32)

        def tile(buf, n):
            return buf[:, n, :] if isinstance(n, int) else buf[:, bass.ds(n, 1), :].rearrange("p a s -> p (a s)")

        def col(buf, n):
            return buf[:, n:n + 1] if isinstance(n, int) else buf[:, bass.ds(n, 1)]

        ident = con[:, C_ID:C_ID + P]
        ones = con[:, C_ONE:C_ONE + P]

        ssum2 = con[:, C_COUNT:C_COUNT + SEQ]
        Q_IN, Q_FFN0, Q_MID, Q_FFN1, Q_FIN, Q_VAR, Q_FFN2, Q_OUT = range(8)
        S_IN, S_FFN0, S_MID, S_FFN1, S_FIN, S_MIX2, S_MEAN, S_VAR, S_FFN2, S_OUT = range(10)

        @block.sync
        def _(eng):
            def load(u, s):
                wait(eng, w_lo, 2 * (u - 1) + s + 1)
                g = 2 * u + s
                src = stream[g] if isinstance(g, int) else stream[bass.ds(g, 1)].rearrange("a p k c -> (a p) k c")
                eng.dma_start(raw[s][:, :, :], src).then_inc(landed[s], 16)

            eng.dma_start(vec[:, :], vec_d).then_inc(in_vec, 16)
            load(0, 0)
            for n in range(KD):
                eng.dma_start(h[:, n, :], x_t[:, n, :]).then_inc(in_h[n], 16)
                if n == 1:
                    load(0, 1)
            eng.dma_start(con[:, :], const_d).then_inc(in_con, 16)
            def load_ada(j, s):
                wait(eng, ada_sum, j - 1)
                src = ada_w[j] if isinstance(j, int) else ada_w[bass.ds(j, 1)].rearrange("a p k c -> (a p) k c")
                eng.dma_start(araw[s][:, :, :], src).then_inc(ada_land[s], 16)

            at = 1
            for which in range(2):
                u, j = U_FFN[which], ADA_TILES * which
                with eng.Fori(at, u) as v:
                    load(v, 0)
                    load(v, 1)

                def beside_up(w, u=u, j=j):
                    for s in range(2):
                        load(2 * w + u + s, 0)
                        load(2 * w + u + s, 1)
                        load_ada(2 * w + j + s, s)
                loop(eng, 0, PARTS[0] // 2, beside_up, peel=which == 0)
                u, j = u + PARTS[0], j + PARTS[0]
                with eng.Fori(0, KD // 2) as w:
                    for s in range(2):
                        load(w + u, s)
                        load_ada(2 * w + j + s, s)
                u, j = u + KD // 2, j + KD
                with eng.Fori(0, PARTS[1] // 2) as w:
                    beside_up(w, u, j)
                at = u + PARTS[1]
            with eng.Fori(at, U_END) as v:
                load(v, 0)
                load(v, 1)
            for n in range(KD):
                eng.wait_ge(done, n + 1)
                eng.dma_start(out_t[:, n, :], h[:, n, :]).then_inc(stored, 16)
            eng.wait_ge(stored, 16 * KD)

        @block.scalar
        def _(eng):
            def split_hi(u, s):
                if isinstance(u, int) and u >= U_END:
                    return
                wait(eng, landed[s], 16 * (u + 1))
                wait(eng, used, 2 * (u - 1) + s + 1)
                eng.activation(wh[s][:, :, :], raw[s][:, :, :], ACT.Copy).then_inc(w_hi, 1)

            def square(n, s, count, src, ready, value):
                wait_apart(eng, ready, value, passed)
                if not isinstance(count, int) or count > 1:
                    wait_apart(eng, sq_added, count - 1, passed)
                eng.activation(sq[s][:, :], tile(src, n), ACT.Square).then_inc(sq_ready, 1)

            def residual(u0, rnd, gains=None, gains2=None, gains_sq=None, last=False):
                def pair(u):
                    for s in range(2):
                        n = 2 * (u - u0) + s
                        split_hi(u + 1, s)
                        wait_apart(eng, evac[s], u + 1, passed)
                        if gains is not None:
                            eng.activation(tile(xh, n), tile(h, n), ACT.Copy,
                                           scale=col(vec, gains + n)).then_inc(x_hi, 1)
                        if gains2 is not None:
                            eng.activation(tile(x2h, n), tile(h, n), ACT.Copy,
                                           scale=col(vec, gains2 + n)).then_inc(x2_hi, 1)
                        square(n, s, 8 * rnd + n, h, evac[s], u + 1)
                        if gains_sq is not None:
                            wait_apart(eng, sq2_added, n + 1, passed)
                            eng.activation(tmp[s][:, :], tile(h, n), ACT.Square,
                                           scale=col(vec, gains_sq + n)).then_inc(sq2_ready, 1)
                with eng.Fori(u0, u0 + KD // 2 - last) as u:
                    pair(u)
                if last:
                    pair(u0 + KD // 2 - 1)

            def attention(layer):
                base = PAIRS * layer

                def slot(i, par, gemm=True, attn=True):
                    p = 2 * i + par
                    a, gp = p - 1, p + base

                    def step(j):
                        g = 3 * par + j
                        return U_QKV[layer] + 3 * i + g // 2, g % 2

                    def split(j):
                        if gemm:
                            u, s = step(j)
                            split_hi(u + 1, s)

                    def scores_a(hh):
                        n = 3 * (2 * a + hh)
                        for c, (lo, hi) in enumerate(CHUNKS):
                            eng.wait_ge(z_done, n + c + 1)
                            eng.activation(ez[:, lo:hi], Z[c][:, 0:hi - lo], ACT.Abs).then_inc(z_abs, 1)
                        for c, (lo, hi) in enumerate(CHUNKS):
                            eng.wait_ge(z_abs, n + c + 1)
                            eng.activation(ez[:, lo:hi], ez[:, lo:hi], ACT.Exp, scale=-1.0).then_inc(z_exp, 1)
                        for c, (lo, hi) in enumerate(CHUNKS):
                            eng.wait_ge(z_exp, n + c + 1)
                            eng.activation(ez[:, lo:hi], ez[:, lo:hi], ACT.Ln, bias=1.0).then_inc(z_ln, 1)

                    def weights_a(hh):
                        n = 3 * (2 * a + hh)
                        for c, (lo, hi) in enumerate(CHUNKS):
                            eng.wait_ge(cum, n + c + 1)
                            eng.activation(wa[:, lo:hi], Z[c][:, 0:hi - lo], ACT.Exp).then_inc(w_exp, 1)

                    def exp_b(hh):
                        eng.wait_ge(zneg, 2 * a + hh + 1)
                        for b in range(NB):
                            o, w = OFF_Q[b], BLK * (b + 1)
                            eng.activation(ez[:, o:o + w], sp[:, o:o + w], ACT.Exp, bias=small[:, 4 + b:5 + b],
                                           accum_out=small[:, 8 + b:9 + b]).then_inc(p_exp, 1)

                    def copy_b(hh):
                        for c in (0, 2):
                            lo, hi = CHUNKS[c]
                            eng.wait_ge(p_tr, 3 * (2 * a + hh) + c + 1)
                            eng.activation(sp[:, lo:hi], Z[c][:, 0:hi - lo], ACT.Copy).then_inc(p_cp_a, 1)

                    def copy_hi(dst, j):
                        if layer == 0:
                            u, s = step(j)
                            eng.wait_ge(evac[s], u + 1)
                        else:
                            eng.wait_ge(roped, 2 * p + j + 1)
                        eng.activation(dst[par][:, :], qkv[j][:, :], ACT.Copy).then_inc(qk_hi, 1)

                    def values():
                        eng.wait_ge(v_tr, gp)
                        eng.activation(vn[1 - par][:, :, :].rearrange("p b d -> p (b d)"), T[:, :],
                                       ACT.Copy).then_inc(v_nat, 1)

                    def out_hi():
                        wait_apart(eng, pv_done, 2 * gp, passed)
                        eng.activation(tile(yh, a), O[:, :], ACT.Copy).then_inc(o_hi, 1)

                    if layer == 0:
                        if attn:
                            scores_a(0)
                        split(0)
                        if attn:
                            weights_a(0)
                            values()
                        if gemm:
                            copy_hi(qh, 0)
                        if attn:
                            scores_a(1)
                        split(1)
                        if gemm:
                            copy_hi(kh, 1)
                        if attn:
                            weights_a(1)
                        split(2)
                        if attn:
                            out_hi()
                    else:
                        if attn:
                            exp_b(0)
                            values()
                        split(0)
                        if attn:
                            copy_b(0)
                        if gemm:
                            copy_hi(qh, 0)
                        if attn:
                            exp_b(1)
                        split(1)
                        if attn:
                            copy_b(1)
                        split(2)
                        if gemm:
                            copy_hi(kh, 1)
                        if attn:
                            out_hi()

                slot(0, 0, attn=False)
                with eng.Fori(0, PAIRS // 2 - 1) as i:
                    slot(i, 1)
                    slot(i + 1, 0)
                slot(PAIRS // 2 - 1, 1)
                slot(PAIRS // 2, 0, gemm=False)

            def ffn(which, hid, last):
                u, f = U_FFN[which], FT * which
                for part, nt in enumerate(PARTS):
                    with eng.Fori(u, u + nt) as v:
                        n = v - u
                        split_hi(v + 1, 0)
                        if which < 2:
                            eng.wait_ge(evac[0], v + 1)
                            eng.activation(si[:, :], gs[:, :], ACT.Silu).then_inc(silu, 1)
                            split_hi(v + 1, 1)
                            wait_apart(eng, a_raw, n + f + 1, passed)
                            eng.activation(tile(hid, n), af[:, :], ACT.Copy).then_inc(a_hi, 1)
                        else:
                            eng.wait_ge(used, 2 * v + 1)
                            eng.wait_ge(evac[1], v)
                            eng.activation(sgt[:, :], G[0][:, :], ACT.Silu).then_inc(evac[0], 1)
                            split_hi(v + 1, 1)
                            wait_apart(eng, evac[1], v + 1, passed)
                            eng.activation(tile(hid, n), csb[:, :], ACT.Copy).then_inc(a_hi, 1)
                    u, f = u + nt, f + nt
                    if part < len(PARTS) - 1:
                        with eng.Fori(u, u + KD // 2) as v:
                            split_hi(v + 1, 0)
                            split_hi(v + 1, 1)
                    else:
                        last(u)
                    u += KD // 2

            def modulated(shift, dst, before):
                with eng.Fori(0, KD // 2) as i:
                    for s in range(2):
                        n = 2 * i + s
                        wait_apart(eng, mod_t, n + before + 1, passed)
                        eng.activation(tile(dst, n), tmp[s][:, :], ACT.Identity,
                                       bias=col(modc, shift + n)).then_inc(x_hi, 1)

            eng.wait_ge(in_vec, 16)
            eng.activation(cs[:, :], vec[:, V_C:V_C + KD], ACT.Silu).then_inc(cs_ready, 1)
            for n in range(KD):
                if n < 2:
                    split_hi(0, n)
                eng.wait_ge(in_h[n], 16)
                eng.activation(xh[:, n, :], h[:, n, :], ACT.Copy,
                               scale=vec[:, V_MIX0 + n:V_MIX0 + n + 1]).then_inc(x_hi, 1)
                square(n, n % 2, n, h, in_h[n], 16)
            eng.preload_act_table_set("natural_log_exp_and_others")
            attention(0)
            residual(U_WO[0], Q_FFN0, V_FFN0)
            ffn(0, yh, lambda u: residual(u, Q_MID, V_MIX1, V_KV))
            eng.preload_act_table_set("natural_log_exp_and_others")
            attention(1)
            residual(U_WO[1], Q_FFN1, V_FFN1)
            ffn(1, yh, lambda u: residual(u, Q_FIN, gains_sq=V_FIN))
            modulated(M_SH1, xh, 0)
            with eng.Fori(U_CONF, U_CONF + KD) as u:
                split_hi(u + 1, 0)
                eng.wait_ge(used, 2 * u + 1)
                eng.wait_ge(evac[1], u)
                eng.activation(sgt[:, :], G[0][:, :], ACT.Sigmoid).then_inc(evac[0], 1)
                split_hi(u + 1, 1)
            with eng.Fori(0, KD // 2) as i:
                for par in range(2):
                    def step(j):
                        g = 3 * par + j
                        return U_SHORT + 3 * i + g // 2, g % 2
                    u, s = step(0)
                    split_hi(u + 1, s)
                    eng.wait_ge(used, 2 * u + s + 1)
                    up, sp_ = step(-2)
                    eng.wait_ge(evac[sp_], up + 1)
                    eng.activation(csb[:, :], G[s][:, :], ACT.Copy).then_inc(evac[s], 1)
                    for j in (1, 2):
                        u, s = step(j)
                        split_hi(u + 1, s)
                    wait_apart(eng, evac[s], u + 1, passed)
                    eng.activation(tile(yh, 2 * i + par), sq[0][:, :], ACT.Copy).then_inc(s_hi, 1)
            with eng.Fori(U_GA, U_GA + KD) as u:
                split_hi(u + 1, 0)
                eng.wait_ge(used, 2 * u + 1)
                eng.wait_ge(evac[1], u)
                eng.activation(sgt[:, :], G[0][:, :], ACT.Sigmoid).then_inc(evac[0], 1)
                split_hi(u + 1, 1)
            def split_b(n):
                split_hi(U_GB + n // 2 + 1, n % 2)

            def gate_b(n):
                u, s = U_GB + n // 2, n % 2
                eng.wait_ge(used, 2 * u + s + 1)
                eng.activation(sgb[:, n, :], G[s][:, :], ACT.Sigmoid).then_inc(evac[s], 1)

            def ln_hi(n):
                eng.wait_ge(ln_t, n + 1)
                eng.activation(acc[:, n, :], acc[:, n, :], ACT.Silu, scale=vec[:, V_LG + n:V_LG + n + 1],
                               bias=vec[:, V_LB + n:V_LB + n + 1]).then_inc(ln_s, 1)
                eng.wait_ge(ln_s, n + 1)
                eng.activation(yh[:, n, :], acc[:, n, :], ACT.Copy).then_inc(u_hi, 1)

            for n in range(4):
                if n < 2:
                    for m in range(4 * n, 4 * n + 4):
                        square(m, m % 2, 8 * Q_VAR + m, acc, centred, m + 1)
                split_b(n)
                gate_b(n)
            for n in range(KD):
                ln_hi(n)
                if n % 4 == 2:
                    split_b(4 + n // 4 * 2)
                if n % 4 == 3:
                    gate_b(4 + n // 4 * 2)
                    split_b(5 + n // 4 * 2)
                    gate_b(5 + n // 4 * 2)
            with eng.Fori(U_CO, U_CO + KD // 2) as u:
                for s in range(2):
                    n = 2 * (u - U_CO) + s
                    split_hi(u + 1, s)
                    wait_apart(eng, mix_t, n + 1, passed)
                    eng.activation(tile(xh, n), tmp[s][:, :], ACT.Copy).then_inc(mix_hi, 1)
            residual(U_OUT, Q_FFN2)
            modulated(M_SH2, yh, KD)
            ffn(2, xh, lambda u: residual(u, Q_OUT, last=True))

        @block.vector
        def _(eng):
            def split_lo(u, s):
                if isinstance(u, int) and u >= U_END:
                    return
                eng.wait_ge(w_hi, 2 * u + s + 1)
                eng.tensor_tensor(wl[s][:, :, :], raw[s][:, :, :], f32(wh[s][:, :, :]), ALU.subtract).then_inc(w_lo, 1)

            def operand_lo(hi, lo, n, gain, hi_sem, lo_sem, count):
                eng.wait_ge(hi_sem, count + 1)
                eng.scalar_tensor_tensor(tile(lo, n), tile(h, n), gain, f32(tile(hi, n)), ALU.mult,
                                         ALU.subtract).then_inc(lo_sem, 1)

            def residual(u0, gate=None, x_before=None, x2_before=None, gains=None, gains2=None, last=False):
                def pair(u):
                    for s in range(2):
                        n = 2 * (u - u0) + s
                        eng.wait_ge(used, 2 * u + s + 1)
                        if gate is None:
                            eng.tensor_tensor(tile(h, n), G[s][:, :], tile(h, n), ALU.add).then_inc(evac[s], 1)
                        else:
                            eng.scalar_tensor_tensor(tile(h, n), G[s][:, :], col(modc, gate + n), tile(h, n),
                                                     ALU.mult, ALU.add).then_inc(evac[s], 1)
                        split_lo(u + 1, s)
                        if gains is not None:
                            eng.wait_ge(evac[s], u + 1)
                            operand_lo(xh, xl, n, col(vec, gains + n), x_hi, x_lo, x_before + n)
                        if gains2 is not None:
                            operand_lo(x2h, x2l, n, col(vec, gains2 + n), x2_hi, x2_lo, x2_before + n)
                with eng.Fori(u0, u0 + KD // 2 - last) as u:
                    pair(u)
                if last:
                    pair(u0 + KD // 2 - 1)

            def statistic(idx, eps, between=None):
                r = idx - (idx > S_MEAN)
                eng.wait_ge(stat, idx + 1)
                eng.tensor_scalar(var4[:, :], O[:, 0:NB], 1.0 / D, eps, ALU.mult, ALU.add).then_inc(var_ready, 1)
                eng.wait_ge(root_ready, r + 1)
                eng.tensor_tensor(tmp[0][:, :].rearrange("p (b t) -> p b t", b=NB),
                                  ident.unsqueeze(1).to_broadcast([P, NB, P]),
                                  root4[:, :].unsqueeze(2).to_broadcast([P, NB, P]), ALU.mult).then_inc(diag_ready, 1)
                if between is not None:
                    split_lo(*between)
                eng.wait_ge(spread, r + 1)
                eng.tensor_copy(rstd[:, :], O[:, :]).then_inc(rstd_ready, 1)

            def attention(layer):
                base = PAIRS * layer

                def slot(i, par, gemm=True, attn=True):
                    p = 2 * i + par
                    a, gp = p - 1, p + base

                    def step(j):
                        g = 3 * par + j
                        return U_QKV[layer] + 3 * i + g // 2, g % 2

                    def project(j):
                        u, s = step(j)
                        eng.wait_ge(used, 2 * u + s + 1)
                        if j < 2:
                            wait(eng, qk_lo, 2 * gp)
                        else:
                            wait(eng, v_tr, gp)
                        if j == 0:
                            eng.scalar_tensor_tensor(qkv[j][:, :], G[s][:, :], HD ** -0.5, rstd[:, :], ALU.mult,
                                                     ALU.mult).then_inc(evac[s], 1)
                        else:
                            eng.tensor_tensor(qkv[j][:, :], G[s][:, :], rstd[:, :], ALU.mult).then_inc(evac[s], 1)
                        split_lo(u + 1, s)

                    def scores_a(hh):
                        n = 3 * (2 * a + hh)
                        for chunks in ((0, 1), (2,)):
                            for c in chunks:
                                lo, hi = CHUNKS[c]
                                eng.wait_ge(z_ln, n + c + 1)
                                eng.scalar_tensor_tensor(sp[:, lo:hi], Z[c][:, 0:hi - lo], 0.0, ez[:, lo:hi], ALU.max,
                                                         ALU.add).then_inc(sp_ready, 1)
                            for c in chunks:
                                lo, hi = CHUNKS[c]
                                eng.wait_ge(sp_ready, n + c + 1)
                                eng.tensor_copy(sph[:, lo:hi], sp[:, lo:hi]).then_inc(sp_hi, 1)
                            for c in chunks:
                                lo, hi = CHUNKS[c]
                                eng.wait_ge(sp_hi, n + c + 1)
                                eng.tensor_tensor(spl[:, lo:hi], sp[:, lo:hi], f32(sph[:, lo:hi]),
                                                  ALU.subtract).then_inc(sp_lo, 1)

                    def maxima_b(hh):
                        n = 2 * a + hh
                        for b in range(NB):
                            o, w = OFF_Q[b], BLK * (b + 1)
                            c = (0, 0, 1, 2)[b]
                            z0 = o - CHUNKS[c][0]
                            wait_apart(eng, z_done, 3 * (2 * (gp - 1) + hh) + c + 1, passed)
                            eng.tensor_tensor_reduce(sp[:, o:o + w], Z[c][:, z0:z0 + w],
                                                     con[:, C_COUNT + o:C_COUNT + o + w], 1.0, -3e38, ALU.add,
                                                     ALU.max, small[:, b:b + 1]).then_inc(zmax, 1)
                        eng.wait_ge(zmax, NB * n + NB)
                        eng.tensor_scalar(small[:, 4:8], small[:, 0:4], -1.0, None, ALU.mult).then_inc(zneg, 1)

                    def inverse_b(hh):
                        n = 2 * a + hh
                        eng.wait_ge(p_exp, NB * n + NB)
                        eng.reciprocal(small[:, 12:16], small[:, 8:12]).then_inc(rden, 1)
                        eng.wait_ge(rden, n + 1)
                        eng.tensor_tensor(sq[hh][:, :].rearrange("p (b t) -> p b t", b=NB),
                                          ident.unsqueeze(1).to_broadcast([P, NB, P]),
                                          small[:, 12:16].unsqueeze(2).to_broadcast([P, NB, P]),
                                          ALU.mult).then_inc(den_diag, 1)

                    def copy_b(hh):
                        lo, hi = CHUNKS[1]
                        eng.wait_ge(p_tr, 3 * (2 * a + hh) + 2)
                        eng.tensor_copy(sp[:, lo:hi], Z[1][:, 0:hi - lo]).then_inc(p_cp_d, 1)

                    def rotate(j):
                        eng.wait_ge(perm, 2 * p + j + 1)
                        eng.tensor_tensor(tmp[j][:, :], T[:, :], con[:, C_SIN:C_SIN + SEQ], ALU.mult).then_inc(rot, 1)

                    def out_lo():
                        eng.wait_ge(o_hi, gp)
                        eng.tensor_tensor(tile(yl, a), O[:, :], f32(tile(yh, a)), ALU.subtract).then_inc(o_lo, 1)

                    if layer == 0:
                        if attn:
                            scores_a(0)
                        if gemm:
                            project(0)
                            project(1)
                        if attn:
                            scores_a(1)
                        if gemm:
                            project(2)
                    else:
                        if attn:
                            maxima_b(0)
                            inverse_b(0)
                        if gemm:
                            project(0)
                            rotate(0)
                        if attn:
                            copy_b(0)
                            maxima_b(1)
                            inverse_b(1)
                        if gemm:
                            project(1)
                            rotate(1)
                        if attn:
                            copy_b(1)
                        if gemm:
                            project(2)
                    if attn:
                        out_lo()

                slot(0, 0, attn=False)
                with eng.Fori(0, PAIRS // 2 - 1) as i:
                    slot(i, 1)
                    slot(i + 1, 0)
                slot(PAIRS // 2 - 1, 1)
                slot(PAIRS // 2, 0, gemm=False)

            def ffn(which, last):
                u, f = U_FFN[which], FT * which
                for part, nt in enumerate(PARTS):
                    def hidden(v):
                        n = v - u
                        if which < 2:
                            eng.wait_ge(used, 2 * v + 1)
                            wait(eng, silu, n + f)
                            eng.tensor_tensor(gs[:, :], G[0][:, :], rstd[:, :], ALU.mult).then_inc(evac[0], 1)
                            if not (isinstance(v, int) and v == U_FFN[which]):
                                split_lo(v + 1, 0)
                            eng.wait_ge(used, 2 * v + 2)
                            wait(eng, a_raw, n + f)
                            eng.tensor_tensor(us[:, :], G[1][:, :], rstd[:, :], ALU.mult).then_inc(evac[1], 1)
                            split_lo(v + 1, 1)
                        else:
                            split_lo(v + 1, 0)
                            eng.wait_ge(used, 2 * v + 2)
                            eng.wait_ge(evac[0], v + 1)
                            eng.wait_ge(a_lo, n + f)
                            eng.tensor_tensor(csb[:, :], G[1][:, :], sgt[:, :], ALU.mult).then_inc(evac[1], 1)
                            split_lo(v + 1, 1)
                    loop(eng, u, u + nt, hidden, peel=which < 2 and part == 0)
                    u, f = u + nt, f + nt
                    if part < len(PARTS) - 1:
                        residual(u, gate=M_G2 if which == 2 else None)
                    else:
                        last(u)
                    u += KD // 2

            def modulated(gm, shift, hi, lo, before, x_before):
                with eng.Fori(0, KD // 2) as i:
                    for s in range(2):
                        n = 2 * i + s
                        eng.wait_ge(x_lo, n + x_before - 1)
                        eng.scalar_tensor_tensor(tmp[s][:, :], tile(h, n), col(gmc, gm + n), rstd[:, :], ALU.mult,
                                                 ALU.mult).then_inc(mod_t, 1)
                    for s in range(2):
                        n = 2 * i + s
                        eng.wait_ge(x_hi, n + x_before + 1)
                        eng.wait_ge(mod_t, n + before + 1)
                        eng.scalar_tensor_tensor(tile(lo, n), tmp[s][:, :], col(modc, shift + n), f32(tile(hi, n)),
                                                 ALU.add, ALU.subtract).then_inc(x_lo, 1)

            def taps(t, part, parts):
                for k in range(-(-ND * part // parts), -(-ND * (part + 1) // parts)):
                    total = tile(acc, t) if k % 2 == 0 else rstd[:, :]
                    weight = col(vec, CONF_K * t + V_CW + k)
                    window = tile(cin[:, :, k:k + SEQ], t)
                    if k == 1:
                        wait(eng, tap_d, NV_OPS * t)
                    if k < 2:
                        eng.tensor_scalar(total, window, weight, None, ALU.mult).then_inc(tap_d, 1)
                    else:
                        eng.wait_ge(tap_d, NV_OPS * t + k - 1)
                        eng.scalar_tensor_tensor(total, window, weight, total, ALU.mult, ALU.add).then_inc(tap_d, 1)

            def conv_end(t):
                eng.wait_ge(tap_d, NV_OPS * t + ND)
                eng.tensor_tensor(tile(acc, t), tile(acc, t), rstd[:, :], ALU.add).then_inc(tap_d, 1)
                eng.wait_ge(tap_p, NP_OPS * t + NP_OPS)
                eng.wait_ge(tap_d, NV_OPS * t + NV_OPS)
                eng.scalar_tensor_tensor(tile(acc, t), tile(acc, t), col(vec, V_CB + t), tmp[0][:, :], ALU.add,
                                         ALU.add).then_inc(u_ready, 1)

            for n in range(KD):
                if n < 2:
                    split_lo(0, n)
                operand_lo(xh, xl, n, vec[:, V_MIX0 + n:V_MIX0 + n + 1], x_hi, x_lo, n)
            eng.wait_ge(in_con, 16)
            for dst, c in ((ntri, C_NTRI), (nones, C_NONE), (idb, C_ID), (maskb, C_MASK)):
                eng.tensor_copy(dst[:, :], con[:, c:c + P]).then_inc(consts, 1)
            statistic(S_IN, EPS)
            eng.wait_ge(rstd_ready, 1)
            attention(0)
            residual(U_WO[0], x_before=KD, gains=V_FFN0)
            statistic(S_FFN0, EPS, between=(U_FFN[0] + 1, 0))
            eng.wait_ge(rstd_ready, 2)
            ffn(0, lambda u: residual(u, x_before=2 * KD, gains=V_MIX1, x2_before=0, gains2=V_KV))
            statistic(S_MID, EPS)
            eng.wait_ge(rstd_ready, 3)
            attention(1)
            residual(U_WO[1], x_before=3 * KD, gains=V_FFN1)
            statistic(S_FFN1, EPS, between=(U_FFN[1] + 1, 0))
            eng.wait_ge(rstd_ready, 4)
            ffn(1, lambda u: residual(u))
            eng.wait_ge(ada_mm, 48)
            eng.tensor_tensor(modc[:, :], M[:, 0:48], vec[:, V_ADA:V_ADA + 48], ALU.add).then_inc(modc_ready, 1)
            eng.wait_ge(modc_ready, 1)
            for at, scale, gain in ((0, M_SC1, V_MIX2), (KD, M_SC2, V_FFN2)):
                eng.scalar_tensor_tensor(gmc[:, at:at + KD], modc[:, scale:scale + KD], 1.0, vec[:, gain:gain + KD],
                                         ALU.add, ALU.mult).then_inc(gmc_ready, 1)
            def diagonal():
                eng.tensor_tensor(tmp[0][:, :].rearrange("p (b t) -> p b t", b=NB),
                                  ident.unsqueeze(1).to_broadcast([P, NB, P]),
                                  root4[:, :].unsqueeze(2).to_broadcast([P, NB, P]), ALU.mult).then_inc(diag_ready, 1)

            def output(n):
                eng.scalar_tensor_tensor(h[:, n, :], h[:, n, :], vec[:, V_FIN + n:V_FIN + n + 1], rstd[:, :],
                                         ALU.mult, ALU.mult).then_inc(y_ready, 1)
            eng.wait_ge(stat, S_MIX2 + 1)
            eng.tensor_scalar(var4[:, :], O[:, 0:NB], 1.0 / D, EPS, ALU.mult, ALU.add).then_inc(var_ready, 1)
            eng.tensor_scalar(mean4[:, :], O[:, NB:2 * NB], 1.0 / D, None, ALU.mult).then_inc(sum2_ready, 1)
            eng.wait_ge(root_ready, S_FIN + 1)
            diagonal()
            eng.wait_ge(sum2_ready, 1)
            eng.tensor_tensor(mean4[:, :], mean4[:, :], root4[:, :], ALU.mult).then_inc(sum2_ready, 1)
            eng.wait_ge(sum2_ready, 2)
            eng.tensor_tensor(mean4[:, :], mean4[:, :], root4[:, :], ALU.mult).then_inc(sum2_ready, 1)
            eng.wait_ge(sum2_ready, 3)
            eng.tensor_scalar(var4[:, :], mean4[:, :], EPS, None, ALU.add).then_inc(var_ready, 1)
            eng.wait_ge(spread, S_FIN + 1)
            eng.tensor_copy(rstd[:, :], O[:, :]).then_inc(rstd_ready, 1)
            eng.wait_ge(rstd_ready, 5)
            for n in range(KD // 2):
                output(n)
            eng.wait_ge(root_ready, S_MIX2 + 1)
            diagonal()
            for n in range(KD // 2, KD):
                output(n)
            eng.wait_ge(y_ready, KD)
            eng.wait_ge(spread, S_MIX2 + 1)
            eng.tensor_copy(rstd[:, :], O[:, :]).then_inc(rstd_ready, 1)
            eng.wait_ge(rstd_ready, 6)
            eng.wait_ge(gmc_ready, 2)
            modulated(0, M_SH1, xh, xl, 0, 4 * KD)
            eng.wait_ge(padded, 2)

            def conf(t):
                for m in range(4):
                    n = 4 * t + m
                    u = U_CONF + n
                    split_lo(u + 1, 0)
                    eng.wait_ge(used, 2 * u + 2)
                    eng.wait_ge(evac[0], u + 1)
                    eng.tensor_tensor(tile(cin[:, :, PADC:], n), G[1][:, :], sgt[:, :], ALU.mult).then_inc(evac[1], 1)
                    split_lo(u + 1, 1)
                    if m == 0:
                        eng.wait_ge(evac[1], U_CONF + t + 1)
                    taps(t, m, 4)
                conv_end(t)
            loop(eng, 0, 2, conf, peel=True)
            eng.wait_ge(evac[1], U_CONF + KD)

            def short(i):
                t = i + 2
                for par in range(2):
                    n = 2 * i + par

                    def step(j):
                        g = 3 * par + j
                        return U_SHORT + 3 * i + g // 2, g % 2
                    u, s = step(0)
                    split_lo(u + 1, s)
                    taps(t, 3 * par, 6)
                    uc, sc = u, s
                    u, s = step(1)
                    eng.wait_ge(evac[sc], uc + 1)
                    eng.wait_ge(used, 2 * u + s + 1)
                    wait(eng, s_lo, n)
                    eng.tensor_tensor(cv[:, PADS:], G[s][:, :], csb[:, :], ALU.mult).then_inc(evac[s], 1)
                    split_lo(u + 1, s)
                    uv, sv = u, s
                    taps(t, 3 * par + 1, 6)
                    for k in range(SHORT_K):
                        weight = col(vec, SHORT_K * n + V_SW + k)
                        if k == 0:
                            eng.wait_ge(evac[sv], uv + 1)
                            eng.tensor_scalar(sq[1][:, :], cv[:, 0:SEQ], weight, None, ALU.mult).then_inc(s_tap, 1)
                        else:
                            eng.wait_ge(s_tap, SHORT_K * n + k)
                            eng.scalar_tensor_tensor(sq[1][:, :], cv[:, k:k + SEQ], weight, sq[1][:, :], ALU.mult,
                                                     ALU.add).then_inc(s_tap, 1)
                    u, s = step(2)
                    eng.wait_ge(s_tap, SHORT_K * n + SHORT_K)
                    eng.wait_ge(used, 2 * u + s + 1)
                    eng.tensor_tensor(sq[0][:, :], G[s][:, :], sq[1][:, :], ALU.mult).then_inc(evac[s], 1)
                    split_lo(u + 1, s)
                    taps(t, 3 * par + 2, 6)
                    eng.wait_ge(s_hi, n + 1)
                    eng.wait_ge(evac[s], u + 1)
                    eng.tensor_tensor(tile(yl, n), sq[0][:, :], f32(tile(yh, n)), ALU.subtract).then_inc(s_lo, 1)
                conv_end(t)
            loop(eng, 0, KD // 2, short, peel=True)
            with eng.Fori(0, 2) as i:
                for m in range(4):
                    t = i + 6
                    n = 4 * i + m
                    u = U_GA + n
                    split_lo(u + 1, 0)
                    if m < 3:
                        taps(t, 2 * m, 6)
                    eng.wait_ge(used, 2 * u + 2)
                    eng.wait_ge(evac[0], u + 1)
                    eng.tensor_tensor(tile(ma, n), G[1][:, :], sgt[:, :], ALU.mult).then_inc(evac[1], 1)
                    split_lo(u + 1, 1)
                    if m < 3:
                        taps(t, 2 * m + 1, 6)
                    if m == 2:
                        conv_end(t)
            eng.wait_ge(stat, S_MEAN + 1)
            eng.tensor_scalar(tmp[0][:, :], O[:, :], 1.0 / D, None, ALU.mult).then_inc(var_ready, 1)
            eng.wait_ge(var_ready, S_MEAN + 1)
            eng.wait_ge(u_ready, KD)
            for n in range(KD):
                eng.tensor_tensor(acc[:, n, :], acc[:, n, :], tmp[0][:, :], ALU.subtract).then_inc(centred, 1)
                if n in (3, 7):
                    split_lo(U_GB + 1, n // 4)
            statistic(S_VAR, LN_EPS, between=(U_GB + 2, 0))
            eng.wait_ge(rstd_ready, 7)
            eng.wait_ge(centred, KD)

            def ln_lo(n):
                eng.wait_ge(u_hi, n + 1)
                eng.tensor_tensor(yl[:, n, :], acc[:, n, :], f32(yh[:, n, :]), ALU.subtract).then_inc(u_lo, 1)

            ahead = 2
            for n in range(KD + ahead):
                if n < KD:
                    eng.tensor_tensor(acc[:, n, :], acc[:, n, :], rstd[:, :], ALU.mult).then_inc(ln_t, 1)
                if n == 1:
                    split_lo(U_GB + 2, 1)
                if n >= ahead:
                    ln_lo(n - ahead)
                if n - ahead == 2:
                    split_lo(U_GB + 3, 0)
                if n - ahead == 3:
                    split_lo(U_GB + 3, 1)
                if n - ahead == 6:
                    split_lo(U_CO, 0)
            split_lo(U_CO, 1)
            eng.wait_ge(evac[1], U_GB)

            def mix(u):
                for s in range(2):
                    n = 2 * (u - U_CO) + s
                    wait(eng, mix_lo, n - 1)
                    eng.wait_ge(used, 2 * u + s + 1)
                    eng.tensor_tensor(tmp[s][:, :], G[s][:, :], tile(sgb, n), ALU.mult).then_inc(evac[s], 1)
                    split_lo(u + 1, s)
                    eng.wait_ge(evac[s], u + 1)
                    eng.tensor_tensor(tmp[s][:, :], tmp[s][:, :], tile(ma, n), ALU.add).then_inc(mix_t, 1)
                    eng.wait_ge(mix_hi, n + 1)
                    eng.tensor_tensor(tile(xl, n), tmp[s][:, :], f32(tile(xh, n)), ALU.subtract).then_inc(mix_lo, 1)
            loop(eng, U_CO, U_CO + KD // 2, mix, peel=True)
            residual(U_OUT, gate=M_G1)
            statistic(S_FFN2, EPS)
            eng.wait_ge(rstd_ready, 8)
            modulated(KD, M_SH2, yh, yl, KD, 5 * KD)
            ffn(2, lambda u: residual(u, gate=M_G2, last=True))
            statistic(S_OUT, EPS)
            eng.wait_ge(rstd_ready, 9)
            for n in range(KD):
                eng.scalar_tensor_tensor(h[:, n, :], h[:, n, :], vec[:, V_FIN2 + n:V_FIN2 + n + 1], rstd[:, :],
                                         ALU.mult, ALU.mult).then_inc(done, 1)

        @block.gpsimd
        def _(eng):
            def clear(count):
                eng.memset(ssum[:, :], 0.0).then_inc(ss_clear, 1)
                eng.wait_ge(ss_clear, count + 1)

            def add_square(s, count):
                eng.wait_ge(sq_ready, count + 1)
                wait(eng, sq_added, count)
                eng.tensor_tensor(ssum[:, :], ssum[:, :], sq[s][:, :], ALU.add).then_inc(sq_added, 1)

            def add_round(rnd, second=False):
                with eng.Fori(0, KD // 2) as i:
                    for s in range(2):
                        add_square(s, 2 * i + s + 8 * rnd)
                        if second:
                            eng.wait_ge(sq2_ready, 2 * i + s + 1)
                            eng.wait_ge(sq2_added, 2 * i + s + 2)
                            eng.tensor_tensor(ssum2, ssum2, tmp[s][:, :], ALU.add).then_inc(sq2_added, 1)

            def inverse_root(idx, cleared):
                eng.wait_ge(var_ready, idx + 1)
                eng.tensor_tensor(root4[:, :], var4[:, :], mhalf[:, 0:1].to_broadcast([P, NB]), ALU.pow)\
                   .then_inc(root_ready, 1)
                clear(cleared)

            def attention(layer):
                base = PAIRS * layer

                def slot(i, par, gemm=True, attn=True):
                    p = 2 * i + par
                    a, gp = p - 1, p + base

                    def lo(dst_h, dst_l, j):
                        eng.wait_ge(qk_hi, 2 * gp + j + 1)
                        eng.tensor_tensor(dst_l[par][:, :], qkv[j][:, :], f32(dst_h[par][:, :]),
                                          ALU.subtract).then_inc(qk_lo, 1)

                    def rotate(j):
                        eng.wait_ge(rot, 2 * p + j + 1)
                        eng.tensor_tensor(qkv[j][:, :], qkv[j][:, :], con[:, C_COS:C_COS + SEQ],
                                          ALU.mult).then_inc(roped_c, 1)
                        eng.wait_ge(roped_c, 2 * p + j + 1)
                        eng.tensor_tensor(qkv[j][:, :], qkv[j][:, :], tmp[j][:, :], ALU.add).then_inc(roped, 1)

                    if layer == 0:
                        if gemm:
                            lo(qh, ql, 0)
                            lo(kh, kl, 1)
                    else:
                        if gemm:
                            rotate(0)
                            lo(qh, ql, 0)
                            rotate(1)
                            lo(kh, kl, 1)

                slot(0, 0, attn=False)
                with eng.Fori(0, PAIRS // 2 - 1) as i:
                    slot(i, 1)
                    slot(i + 1, 0)
                slot(PAIRS // 2 - 1, 1)
                slot(PAIRS // 2, 0, gemm=False)

            def fold_ada(j, s):
                eng.wait_ge(ada_land[s], 8 * (j + 2 - s))
                wait(eng, ada_sum, j)
                eng.tensor_tensor(aprod[:, :, :], araw[s][:, :, :], cs[:, :].unsqueeze(2).to_broadcast([P, KD, P]),
                                  ALU.mult).then_inc(ada_fold, 1)
                for m, half in enumerate((4, 2)):
                    eng.wait_ge(ada_fold, 3 * j + m + 1)
                    eng.tensor_tensor(aprod[:, 0:half, :], aprod[:, 0:half, :], aprod[:, half:2 * half, :],
                                      ALU.add).then_inc(ada_fold, 1)
                eng.wait_ge(ada_fold, 3 * j + 3)
                wait(eng, ada_mm, j - 1)
                eng.tensor_tensor(asum[s][:, :], aprod[:, 0, :], aprod[:, 1, :], ALU.add).then_inc(ada_sum, 1)

            def ffn(which, hid_h, hid_l, rnd):
                f = FT * which

                def hidden(m, part):
                    n = m - f
                    if which < 2:
                        u = U_FFN[which] + sum(PARTS[:part]) + part * (KD // 2)
                        eng.wait_ge(silu, m + 1)
                        eng.wait_ge(evac[1], u + n + 1)
                        wait(eng, a_lo, m)
                        eng.tensor_tensor(af[:, :], si[:, :], us[:, :], ALU.mult).then_inc(a_raw, 1)
                        eng.wait_ge(a_hi, m + 1)
                        eng.tensor_tensor(tile(hid_l, n), af[:, :], f32(tile(hid_h, n)), ALU.subtract)\
                           .then_inc(a_lo, 1)
                    else:
                        eng.wait_ge(a_hi, m + 1)
                        eng.tensor_tensor(tile(hid_l, n), csb[:, :], f32(tile(hid_h, n)), ALU.subtract)\
                           .then_inc(a_lo, 1)

                for part, nt in enumerate(PARTS):
                    j = ADA_TILES * which + (PARTS[0] + KD) * part
                    if which < 2 and part < 2:
                        def with_ada(w):
                            for s in range(2):
                                fold_ada(2 * w + j + s, s)
                                hidden(2 * w + f + s, part)
                        loop(eng, 0, nt // 2, with_ada, peel=f == 0)
                    else:
                        loop(eng, f, f + nt, lambda m: hidden(m, part), peel=f == 0)
                    f += nt
                    if which < 2 and part == 0:
                        with eng.Fori(0, KD // 2) as w:
                            for s in range(2):
                                fold_ada(2 * w + (j + nt) + s, s)
                add_round(rnd, second=which == 1)

            def taps(t):
                for k in range(ND, CONF_K):
                    m = k - ND
                    src = tile(cin[:, :, k:k + SEQ], t)
                    weight = col(vec, CONF_K * t + V_CW + k).to_broadcast([P, SEQ])
                    if m == 0:
                        wait(eng, u_ready, t)
                        eng.tensor_tensor(tmp[0][:, :], src, weight, ALU.mult).then_inc(tap_p, 1)
                    else:
                        before = NP_OPS * t + 2 * m - 1
                        eng.wait_ge(tap_p, before)
                        eng.tensor_tensor(tmp[1][:, :], src, weight, ALU.mult).then_inc(tap_p, 1)
                        eng.wait_ge(tap_p, before + 1)
                        eng.tensor_tensor(tmp[0][:, :], tmp[0][:, :], tmp[1][:, :], ALU.add).then_inc(tap_p, 1)

            def add_u(t):
                eng.wait_ge(u_ready, t + 1)
                wait(eng, u_added, t)
                eng.tensor_tensor(ssum[:, :], ssum[:, :], tile(acc, t), ALU.add).then_inc(u_added, 1)

            eng.memset(mhalf[:, :], -0.5).then_inc(ss_clear, 1)
            clear(1)
            for n in range(KD):
                add_square(n % 2, n)
            inverse_root(S_IN, 2)
            attention(0)
            add_round(Q_FFN0)
            inverse_root(S_FFN0, 3)
            eng.wait_ge(cs_ready, 1)
            ffn(0, yh, yl, Q_MID)
            inverse_root(S_MID, 4)
            attention(1)
            add_round(Q_FFN1)
            eng.memset(ssum2, 0.0).then_inc(sq2_added, 2)
            inverse_root(S_FFN1, 5)
            ffn(1, yh, yl, Q_FIN)
            inverse_root(S_FIN, 6)
            eng.memset(cin[:, :, 0:PADC], 0.0).then_inc(padded, 1)
            eng.memset(cv[:, 0:PADS], 0.0).then_inc(padded, 1)
            inverse_root(S_MIX2, 7)

            def conv(t):
                eng.wait_ge(evac[1], U_CONF + t + 1)
                taps(t)
                add_u(t)
            loop(eng, 0, KD, conv, peel=True)
            eng.wait_ge(var_ready, S_MEAN + 1)
            clear(8)
            add_round(Q_VAR)
            inverse_root(S_VAR, 9)
            add_round(Q_FFN2)
            inverse_root(S_FFN2, 10)
            ffn(2, xh, xl, Q_OUT)
            inverse_root(S_OUT, 11)

        @block.tensor
        def _(eng):
            def product(u, s, src_h, src_l, ready, before, kt=KD, ks=None):
                for k in (range(kt) if ks is None else ks):
                    if k == 0:
                        eng.wait_ge(w_lo, 2 * u + s + 1)
                        wait(eng, evac[s], u)
                    eng.wait_ge(ready, before + k + 1)
                    eng.matmul(G[s][:, :], wh[s][:, k, :], src_h[:, k, :], start=k == 0, stop=False)
                    eng.matmul(G[s][:, :], wh[s][:, k, :], src_l[:, k, :], start=False, stop=False)
                    mm = eng.matmul(G[s][:, :], wl[s][:, k, :], src_h[:, k, :], start=False, stop=k == kt - 1)
                    if k == kt - 1:
                        mm.then_inc(used, 1)

            def steps(u0, pairs, src_h, src_l, ready, before, kt=KD):
                with eng.Fori(u0, u0 + pairs) as u:
                    for s in range(2):
                        product(u, s, src_h, src_l, ready, before, kt)

            def both(u, src_h, src_l, ready, before):
                for k in range(KD):
                    for s in range(2):
                        product(u, s, src_h, src_l, ready, before, ks=[k])

            def statistic(ready, count, total=ssum, at=0):
                eng.wait_ge(ready, count)
                for b in range(NB):
                    mm = eng.matmul(O[:, at + b:at + b + 1], total[:, BLK * b:BLK * b + BLK], ones[:, 0:1],
                                    start=True, stop=True)
                mm.then_inc(stat, 1)

            def spread_root(idx):
                eng.wait_ge(diag_ready, idx - (idx > S_MEAN) + 1)
                eng.matmul(O[:, :], ones, tmp[0][:, :], start=True, stop=True).then_inc(spread, 1)

            def attention(layer):
                base = PAIRS * layer
                x_before = 2 * KD * layer

                def slot(i, par, gemm=True, attn=True):
                    p = 2 * i + par
                    a, gp, ap = p - 1, p + base, 1 - par

                    def step(j):
                        g = 3 * par + j
                        return U_QKV[layer] + 3 * i + g // 2, g % 2

                    def project(lo, hi):
                        if not gemm:
                            for m in range(lo * 14 // 24, hi * 14 // 24):
                                product(U_WO[layer], m // 7, yh, yl, o_lo, base, ks=[m % 7])
                            return
                        for j in range(3):
                            ks = range(max(lo - 8 * j, 0), min(hi - 8 * j, 8))
                            u, s = step(j)
                            if len(ks) == 0:
                                continue
                            if layer == 1 and j > 0:
                                product(u, s, x2h, x2l, x2_lo, 0, ks=ks)
                            else:
                                product(u, s, xh, xl, x_lo, x_before, ks=ks)

                    def scores(hh):
                        rows = slice(HD * hh, HD * hh + HD)
                        if hh == 0:
                            eng.wait_ge(qk_lo, 2 * gp)
                        for c in range(3):
                            if hh == 1 and layer == 0:
                                eng.wait_ge(w_exp, 3 * 2 * a + c + 1)
                            strips = {0: (3, 2), 1: (1,), 2: (0,)}[c] if layer == 0 else {0: (0, 1), 1: (2,), 2: (3,)}[c]
                            for m, b in enumerate(strips):
                                blk = slice(BLK * b, BLK * b + BLK)
                                if layer == 0:
                                    o = OFF_K[b] - CHUNKS[c][0]
                                    w = SEQ - BLK * b
                                    out = Z[c][:, o:o + w]
                                    st, mv = (kh[ap], kl[ap]), (qh[ap], ql[ap])
                                    cols = slice(BLK * b, SEQ)
                                else:
                                    o = OFF_Q[b] - CHUNKS[c][0]
                                    w = BLK * (b + 1)
                                    out = Z[c][:, o:o + w]
                                    st, mv = (qh[ap], ql[ap]), (kh[ap], kl[ap])
                                    cols = slice(0, w)
                                for x, y in ((0, 0), (0, 1), (1, 0)):
                                    mm = eng.matmul(out, st[x][rows, blk], mv[y][rows, cols],
                                                    start=(m == 0 and x == 0 and y == 0), stop=False,
                                                    skip_group_check=True)
                                if layer == 0:
                                    mm = eng.matmul(out[:, 0:BLK], idb[:, :], maskb[:, :], start=False, stop=False,
                                                    skip_group_check=True)
                            mm.then_inc(z_done, 1)

                    def cumulate(hh):
                        n = 3 * (2 * a + hh)
                        for c, strips in enumerate(((3, 2), (1,), (0,))):
                            eng.wait_ge(sp_lo, n + c + 1)
                            for b in strips:
                                o = OFF_K[b] - CHUNKS[c][0]
                                for later in range(b, NB):
                                    w = SEQ - BLK * later
                                    at = o + BLK * (later - b)
                                    for part in (sph, spl):
                                        mm = eng.matmul(Z[c][:, at:at + w], (ntri if later == b else nones)[:, :],
                                                        part[:, OFF_K[later]:OFF_K[later] + w], start=False,
                                                        stop=False, skip_group_check=True)
                            mm.then_inc(cum, 1)

                    def transpose_b(hh):
                        eng.wait_ge(den_diag, 2 * a + hh + 1)
                        for c, strips in enumerate(((3, 2), (1,), (0,))):
                            for b in strips:
                                for q in range(b, NB):
                                    o = OFF_K[b] - CHUNKS[c][0] + BLK * (q - b)
                                    at = OFF_Q[q] + BLK * b
                                    mm = eng.matmul(Z[c][:, o:o + BLK], ez[:, at:at + BLK], sq[hh][:, BLK * q:BLK * q + BLK],
                                                start=True, stop=True)
                            mm.then_inc(p_tr, 1)

                    def weighted(hh):
                        rows = slice(HD * hh, HD * hh + HD)
                        n = 2 * a + hh
                        if hh == 0:
                            eng.wait_ge(v_nat, gp)
                        for b in (3, 2, 1, 0):
                            if layer == 0:
                                eng.wait_ge(w_exp, 3 * n + (3, 2, 1, 1)[b])
                            elif b == 1:
                                eng.wait_ge(p_cp_d, n + 1)
                            else:
                                eng.wait_ge(p_cp_a, 2 * n + (2, 0, 1, 1)[b])
                            w = SEQ - BLK * b
                            src = (wa if layer == 0 else sp)[:, OFF_K[b]:OFF_K[b] + w]
                            mm = eng.matmul(O[rows, BLK * b:SEQ], vn[ap][:, b, rows], src, start=b == 3, stop=b == 0,
                                            skip_group_check=True)
                        mm.then_inc(pv_done, 1)

                    def values():
                        u, s = step(-1)
                        eng.wait_ge(evac[s], u + 1)
                        if layer == 1:
                            eng.wait_ge(rot, 2 * p)
                        for b in range(NB):
                            mm = eng.transpose(T[:, BLK * b:BLK * b + BLK], qkv[2][:, BLK * b:BLK * b + BLK], ident)
                        mm.then_inc(v_tr, 1)

                    def swap(j):
                        u, s = step(j)
                        eng.wait_ge(evac[s], u + 1)
                        if j == 0:
                            wait(eng, v_nat, gp)
                        else:
                            eng.wait_ge(rot, 2 * p + 1)
                        eng.matmul(T[:, :], con[:, C_PERM:C_PERM + P], qkv[j][:, :], start=True, stop=True)\
                           .then_inc(perm, 1)

                    if layer == 0:
                        if attn:
                            scores(0)
                        if attn:
                            project(0, 8)
                        else:
                            both(U_QKV[0], xh, xl, x_lo, 0)
                            eng.wait_ge(in_con, 16)
                            eng.wait_ge(consts, 4)
                            statistic(sq_added, KD)
                            spread_root(S_IN)
                            project(16, 24)
                            return
                        project(8, 10)
                        if attn:
                            cumulate(0)
                            values()
                        project(10, 12)
                        if attn:
                            scores(1)
                            weighted(0)
                        project(12, 22)
                        if attn:
                            cumulate(1)
                        project(22, 24)
                        if attn:
                            weighted(1)
                    else:
                        project(0, 4)
                        if attn:
                            scores(0)
                            values()
                        project(4, 8)
                        if not attn:
                            statistic(sq_added, KD * (Q_MID + 1))
                        project(8, 10)
                        if not attn:
                            spread_root(S_MID)
                        if attn:
                            transpose_b(0)
                        if gemm:
                            swap(0)
                        project(10, 14)
                        if attn:
                            weighted(0)
                            scores(1)
                        project(14, 20)
                        if attn:
                            transpose_b(1)
                        if gemm:
                            swap(1)
                        project(20, 24)
                        if attn:
                            weighted(1)

                slot(0, 0, attn=False)
                with eng.Fori(0, PAIRS // 2 - 1) as i:
                    slot(i, 1)
                    slot(i + 1, 0)
                slot(PAIRS // 2 - 1, 1)
                slot(PAIRS // 2, 0, gemm=False)

            def modulation(j, s):
                eng.wait_ge(ada_sum, j + 1)
                eng.matmul(col(M, j), asum[s][:, :], ones[:, 0:1], start=True, stop=True).then_inc(ada_mm, 1)

            def ffn(which, src_h, src_l, hid_h, hid_l, x_before, stat_idx=None, count=None):
                u, f = U_FFN[which], FT * which
                for part, nt in enumerate(PARTS):
                    j = ADA_TILES * which + (PARTS[0] + KD) * part - 2
                    if part == 0 and stat_idx is not None:
                        product(u, 0, src_h, src_l, x_lo, x_before)
                        statistic(sq_added, count)
                        product(u, 1, src_h, src_l, x_lo, x_before, ks=range(0, 7))
                        spread_root(stat_idx)
                        product(u, 1, src_h, src_l, x_lo, x_before, ks=range(7, KD))
                        steps(u + 1, 1, src_h, src_l, x_lo, x_before)
                    elif part == 0:
                        both(u, src_h, src_l, x_lo, x_before)
                        steps(u + 1, nt - 1, src_h, src_l, x_lo, x_before)
                    if which < 2 and part < 2:
                        with eng.Fori(1 - part, nt // 2) as w:
                            for m in range(2):
                                product(2 * w + u + m, 0, src_h, src_l, x_lo, x_before)
                                modulation(2 * w + j + m, m)
                                product(2 * w + u + m, 1, src_h, src_l, x_lo, x_before)
                    elif part > 0:
                        steps(u, nt, src_h, src_l, x_lo, x_before)
                    u += nt
                    if which < 2 and part == 2:
                        for s in range(2):
                            modulation(ADA_TILES * (which + 1) - 2 + s, s)
                    with eng.Fori(0, KD // 2) as w:
                        for s in range(2):
                            product(w + u, s, hid_h, hid_l, a_lo, f, nt)
                            if which < 2 and part == 0:
                                modulation(2 * w + (j + nt) + s, s)
                    u, f = u + KD // 2, f + nt

            def output(layer):
                for s in range(2):
                    product(U_WO[layer], s, yh, yl, o_lo, PAIRS * layer, ks=[KD - 1])
                steps(U_WO[layer] + 1, 3, yh, yl, o_lo, PAIRS * layer)

            attention(0)
            output(0)
            ffn(0, xh, xl, yh, yl, KD, S_FFN0, KD * (Q_FFN0 + 1))
            attention(1)
            output(1)
            ffn(1, xh, xl, yh, yl, 3 * KD, S_FFN1, KD * (Q_FFN1 + 1))
            statistic(sq_added, KD * (Q_FIN + 1))
            statistic(sq2_added, KD + 2, ssum2, NB)
            spread_root(S_FIN)
            spread_root(S_MIX2)
            both(U_CONF, xh, xl, x_lo, 4 * KD)
            steps(U_CONF + 1, 7 + 12, xh, xl, x_lo, 4 * KD)
            with eng.Fori(U_GA, U_GA + KD - 1) as u:
                product(u, 0, xh, xl, x_lo, 4 * KD)
                product(u, 1, yh, yl, s_lo, 0)
            u = U_GA + KD - 1
            product(u, 0, xh, xl, x_lo, 4 * KD)
            product(u, 1, yh, yl, s_lo, 0, ks=range(0, 4))
            eng.wait_ge(u_added, KD)
            eng.matmul(O[:, :], ones, ssum[:, :], start=True, stop=True).then_inc(stat, 1)
            product(u, 1, yh, yl, s_lo, 0, ks=range(4, KD))
            steps(U_GB, 1, xh, xl, x_lo, 4 * KD)
            u = U_GB + 1
            product(u, 0, xh, xl, x_lo, 4 * KD)
            product(u, 1, xh, xl, x_lo, 4 * KD, ks=range(0, 2))
            statistic(sq_added, KD * (Q_VAR + 1))
            product(u, 1, xh, xl, x_lo, 4 * KD, ks=range(2, KD))
            spread_root(S_VAR)
            steps(u + 1, 2, xh, xl, x_lo, 4 * KD)
            both(U_CO, yh, yl, u_lo, 0)
            steps(U_CO + 1, 3, yh, yl, u_lo, 0)
            steps(U_OUT, 4, xh, xl, mix_lo, 0)
            statistic(sq_added, KD * (Q_FFN2 + 1))
            spread_root(S_FFN2)
            ffn(2, yh, yl, xh, xl, 5 * KD)
            statistic(sq_added, KD * (Q_OUT + 1))
            spread_root(S_OUT)


def tiles(w):
    k, n = w.shape
    return w.reshape(k // P, P, n // P, P).transpose(2, 1, 0, 3)


def ffn_tiles(gate, up, down):
    g, u, at = tiles(gate), tiles(up), 0
    out = []
    for nt in PARTS:
        out.append(np.stack([g[at:at + nt], u[at:at + nt]], 1).reshape(2 * nt, P, KD, P))
        d = np.zeros((KD, P, KD, P), down.dtype)
        d[:, :, 0:nt] = tiles(down[at * P:(at + nt) * P])
        out.append(d)
        at += nt
    return out


def columns(v):
    return v.reshape(-1, P).T


def kernel(**inp):
    import concourse.bacc as bacc
    from concourse.bass_utils import run_bass_kernel_spmd

    a = {k: np.asarray(v) for k, v in inp.items()}
    turn = lambda *ts: np.stack(ts, 1).reshape(-1, P, KD, P)
    qkv_a, kv = tiles(a["w_qkv_a"][0]), tiles(a["w_kv"])
    w_in = tiles(a["w_in_2"][0])
    b_s, c_s, v_s, v_c, gl_c, g_a, g_b = [w_in[KD * i:KD * i + KD] for i in range(7)]
    stream = np.concatenate(
        [turn(qkv_a[0:8], qkv_a[8:16], qkv_a[16:24]), tiles(a["w_o_a"][0])]
        + ffn_tiles(a["w_gate"][0], a["w_up"][0], a["w_down"][0])
        + [turn(tiles(a["w_q_b"][0]), kv[0:8], kv[8:16]), tiles(a["w_o_b"][0])]
        + ffn_tiles(a["w_gate"][1], a["w_up"][1], a["w_down"][1])
        + [turn(gl_c, v_c), turn(c_s, v_s, b_s), turn(g_a, tiles(a["w_short_out_2"][0])), g_b,
           tiles(a["w_conf_out_2"][0]), tiles(a["w_o_2"][0])]
        + ffn_tiles(a["w_ffn_in_2"][0][:, :DFF], a["w_ffn_in_2"][0][:, DFF:], a["w_ffn_out_2"][0]))
    assert stream.shape[0] == 2 * U_END
    vectors = np.concatenate(
        [columns(v) for v in (
            a["norm_mix"][0], a["norm_mix"][1], a["norm_kv"], a["norm_ffn"][0], a["norm_ffn"][1], a["norm_final"],
            a["norm_mix_g_2"][0], a["conv_conf_b_2"][0], a["conf_ln_g_2"][0], a["conf_ln_b_2"][0],
            a["norm_ffn_g_2"][0], a["final_norm_g_2"], a["c_2"][0], a["b_ada_2"][0])]
        + [w.reshape(k, KD, P).transpose(2, 1, 0).reshape(P, KD * k)
           for w, k in ((a["conv_short_w_2"][0], SHORT_K), (a["conv_conf_w_2"][0], CONF_K))], 1)
    arrays = {
        "x_t": a["x"][0].T.reshape(KD, P, SEQ).transpose(1, 0, 2),
        "const_d": constants(),
        "vec_d": vectors,
        "stream": stream,
        "ada_w": tiles(a["w_ada_2"][0]),
    }
    arrays = {k: np.ascontiguousarray(v) for k, v in arrays.items()}
    nc = bacc.Bacc("TRN2", target_bir_lowering=False, num_devices=1)
    args = [nc.dram_tensor(k, list(v.shape), F32, kind="ExternalInput").ap() for k, v in arrays.items()]
    args.append(nc.dram_tensor("out_t", [P, KD, SEQ], F32, kind="ExternalOutput").ap())
    build_program(nc, *args)
    got = run_bass_kernel_spmd(nc, [arrays], core_ids=[0]).results[0]["out_t"]
    return got.transpose(1, 0, 2).reshape(D, SEQ).T.reshape(1, SEQ, D)
```
